# Optimizing a Trainium2 kernel written in Bass

```python
import math
import jax, jax.numpy as jnp
from jax import lax
import numpy as np

D_MODEL = 1024
BATCH = 1
SEQ = 512
DEPTH = 1

HG_HEADS = 4
HG_HEAD_K = 128
HG_HEAD_V = 128
HG_KEY = HG_HEADS * HG_HEAD_K
HG_VAL = HG_HEADS * HG_HEAD_V
GLA_HEADS = 4
GLA_HEAD_K = 64
GLA_HEAD_V = 128
GLA_KEY = GLA_HEADS * GLA_HEAD_K
GLA_VAL = GLA_HEADS * GLA_HEAD_V
GLA_GATE_RANK = 16
GLA_GATE_NORMALIZER = 16.0
MIX_WIDTH = HG_VAL + GLA_VAL
IN_SPLITS = (HG_KEY, HG_KEY, HG_VAL, HG_VAL, GLA_KEY, GLA_KEY, GLA_VAL, GLA_GATE_RANK, GLA_VAL)
IN_WIDTH = sum(IN_SPLITS)
CHUNK = 64
PEER_HEADS = 8
PEER_N_KEYS = 128
PEER_N_EXPERTS = PEER_N_KEYS * PEER_N_KEYS
PEER_QUERY_DIM = 256
PEER_HALF = PEER_QUERY_DIM // 2
PEER_TOPK = 16
PEER_BLOCK = 128
EPS = 1e-6


def rms_norm(x, g):
    xf = x.astype(jnp.float32)
    y = xf * lax.rsqrt(jnp.mean(xf * xf, axis=-1, keepdims=True) + EPS)
    return (y * g.astype(jnp.float32)).astype(x.dtype)

def split_heads(a, n_heads):
    b, t, w = a.shape
    return a.reshape(b, t, n_heads, w // n_heads).transpose(0, 2, 1, 3)

def merge_heads(a):
    b, n, t, d = a.shape
    return a.transpose(0, 2, 1, 3).reshape(b, t, n * d)

def chunk_gated_linear_attention(q, k, v, log_g):
    b, h, t, dk = q.shape
    dv = v.shape[-1]
    n_chunks = t // CHUNK

    def to_chunks(a):
        return a.astype(jnp.float32).reshape(b, h, n_chunks, CHUNK, a.shape[-1]).transpose(2, 0, 1, 3, 4)

    qc, kc, vc, gc = to_chunks(q), to_chunks(k), to_chunks(v), to_chunks(log_g)
    causal = jnp.tril(jnp.ones((CHUNK, CHUNK), dtype=bool))[:, :, None]

    def step(state, inp):
        qb, kb, vb, gb = inp
        cum = jnp.cumsum(gb, axis=2)
        rel = cum[:, :, :, None, :] - cum[:, :, None, :, :]
        decay = jnp.exp(jnp.where(causal, rel, -jnp.inf))
        scores = jnp.einsum('bhid,bhjd,bhijd->bhij', qb, kb, decay)
        out = (jnp.einsum('bhij,bhjv->bhiv', scores, vb)
               + jnp.einsum('bhid,bhdv->bhiv', qb * jnp.exp(cum), state))
        last = cum[:, :, -1:, :]
        state = (jnp.exp(last[:, :, 0, :])[..., None] * state
                 + jnp.einsum('bhjd,bhjv->bhdv', kb * jnp.exp(last - cum), vb))
        return state, out

    s0 = jnp.zeros((b, h, dk, dv), jnp.float32)
    _, o = lax.scan(step, s0, (qc, kc, vc, gc))
    return o.transpose(1, 2, 0, 3, 4).reshape(b, h, t, dv)

def hgrn2_mixer(q, f, i, gate, lower_bound, norm_g):
    q = jax.nn.silu(q)
    forget = lower_bound + (1.0 - lower_bound) * jax.nn.sigmoid(f.astype(jnp.float32))
    key = 1.0 - forget
    log_f = jnp.log(forget)
    o = chunk_gated_linear_attention(split_heads(q, HG_HEADS), split_heads(key, HG_HEADS),
                                     split_heads(i, HG_HEADS), split_heads(log_f, HG_HEADS))
    o = merge_heads(rms_norm(o, norm_g))
    return (o * jax.nn.silu(gate.astype(jnp.float32))).astype(gate.dtype)

def gla_mixer(q, k, v, gate_low, gate, w_gate_up, b_gate, norm_g):
    log_g = jax.nn.log_sigmoid((gate_low @ w_gate_up + b_gate).astype(jnp.float32)) / GLA_GATE_NORMALIZER
    q = q * (GLA_HEAD_K ** -0.5)
    o = chunk_gated_linear_attention(split_heads(q, GLA_HEADS), split_heads(k, GLA_HEADS),
                                     split_heads(v, GLA_HEADS), split_heads(log_g, GLA_HEADS))
    o = merge_heads(rms_norm(o, norm_g))
    return (o * jax.nn.silu(gate.astype(jnp.float32))).astype(gate.dtype)

def peer_ffn(xn, w_q, sub_keys, u, v):
    b, t, d = xn.shape
    blocks = xn.reshape(-1, PEER_BLOCK, d)

    def block(xb):
        q = (xb @ w_q).reshape(PEER_BLOCK, PEER_HEADS, 2, PEER_HALF)
        s = jnp.einsum('thpd,hpnd->thpn', q, sub_keys).astype(jnp.float32)
        s_top, i_top = lax.top_k(s, PEER_TOPK)
        cand = s_top[:, :, 0, :, None] + s_top[:, :, 1, None, :]
        cand_idx = i_top[:, :, 0, :, None] * PEER_N_KEYS + i_top[:, :, 1, None, :]
        cand = cand.reshape(PEER_BLOCK, PEER_HEADS, PEER_TOPK * PEER_TOPK)
        cand_idx = cand_idx.reshape(PEER_BLOCK, PEER_HEADS, PEER_TOPK * PEER_TOPK)
        best, pos = lax.top_k(cand, PEER_TOPK)
        expert = jnp.take_along_axis(cand_idx, pos, axis=-1)
        g = jax.nn.softmax(best, axis=-1)
        act = jax.nn.gelu(jnp.einsum('td,thkd->thk', xb, u[expert]), approximate=False)
        return jnp.einsum('thk,thkd->td', (g * act).astype(xb.dtype), v[expert])

    return lax.map(block, blocks).reshape(b, t, d)

def first_inputs(seed: int = 0) -> dict:
    key = jax.random.key(seed)
    ks = jax.random.split(key, 16)
    nrm = jax.random.normal
    L = DEPTH
    return {
        "x": nrm(ks[0], (BATCH, SEQ, D_MODEL), jnp.float32),
        "norm1_g": 1.0 + 0.02 * nrm(ks[1], (L, D_MODEL), jnp.float32),
        "w_in": nrm(ks[2], (L, D_MODEL, IN_WIDTH), jnp.float32) * D_MODEL ** -0.5,
        "hg_lower_logits": 0.1 * nrm(ks[3], (L + 1, HG_KEY), jnp.float32),
        "hg_norm_g": 1.0 + 0.02 * nrm(ks[4], (L, HG_HEAD_V), jnp.float32),
        "gla_w_gate_up": nrm(ks[5], (L, GLA_GATE_RANK, GLA_KEY), jnp.float32) * GLA_GATE_RANK ** -0.5,
        "gla_b_gate": 0.1 * nrm(ks[6], (L, GLA_KEY), jnp.float32),
        "gla_norm_g": 1.0 + 0.02 * nrm(ks[7], (L, GLA_HEAD_V), jnp.float32),
        "w_out": nrm(ks[8], (L, MIX_WIDTH, D_MODEL), jnp.float32) * MIX_WIDTH ** -0.5,
        "norm2_g": 1.0 + 0.02 * nrm(ks[9], (L, D_MODEL), jnp.float32),
        "peer_w_q": nrm(ks[10], (L, D_MODEL, PEER_HEADS * PEER_QUERY_DIM), jnp.float32) * D_MODEL ** -0.5,
        "peer_sub_keys": nrm(ks[11], (L, PEER_HEADS, 2, PEER_N_KEYS, PEER_HALF), jnp.float32) * PEER_HALF ** -0.5,
        "peer_u": nrm(ks[12], (L, PEER_N_EXPERTS, D_MODEL), jnp.float32) * D_MODEL ** -0.5,
        "peer_v": nrm(ks[13], (L, PEER_N_EXPERTS, D_MODEL), jnp.float32) * 0.3,
        "norm_f_g": 1.0 + 0.02 * nrm(ks[14], (D_MODEL,), jnp.float32),
    }

def first_block(x, norm1_g, w_in, hg_lower_logits, hg_norm_g, gla_w_gate_up, gla_b_gate, gla_norm_g,
              w_out, norm2_g, peer_w_q, peer_sub_keys, peer_u, peer_v, norm_f_g):
    lower_bounds = jnp.cumsum(jax.nn.softmax(hg_lower_logits.astype(jnp.float32), axis=0), axis=0)
    offsets = [int(o) for o in np.cumsum(IN_SPLITS)[:-1]]
    h = x
    for layer in range(DEPTH):
        xn = rms_norm(h, norm1_g[layer])
        proj = xn @ w_in[layer]
        hq, hf, hi, hgate, gq, gk, gv, glow, ggate = jnp.split(proj, offsets, axis=-1)
        o_hgrn = hgrn2_mixer(hq, hf, hi, hgate, lower_bounds[layer], hg_norm_g[layer])
        o_gla = gla_mixer(gq, gk, gv, glow, ggate, gla_w_gate_up[layer], gla_b_gate[layer], gla_norm_g[layer])
        mixed = jnp.concatenate([o_hgrn, o_gla], axis=-1)
        h = h + (mixed @ w_out[layer]).astype(h.dtype)
        hn = rms_norm(h, norm2_g[layer])
        h = h + peer_ffn(hn, peer_w_q[layer], peer_sub_keys[layer], peer_u[layer], peer_v[layer]).astype(h.dtype)
    return rms_norm(h, norm_f_g)


D_MIX = D_MODEL
HEAD_DIM = 64
RET_WIDTH = D_MIX // 2
SB_WIDTH = D_MIX - RET_WIDTH
N_RET_HEADS = RET_WIDTH // HEAD_DIM
N_SB_HEADS = SB_WIDTH // HEAD_DIM
RET_CHUNK = 128
SB_BLOCK = 128
ROPE_BASE = 10000.0
IN_COLS = 4 * RET_WIDTH + 3 * SB_WIDTH
N_KEYS = 128
N_EXPERTS = N_KEYS * N_KEYS
PEER_QDIM = 256
PEER_HALF_2 = PEER_QDIM // 2


def rms_norm_2(x, gain):
    xf = x.astype(jnp.float32)
    y = xf * lax.rsqrt(jnp.mean(xf * xf, axis=-1, keepdims=True) + EPS)
    return (y * gain.astype(jnp.float32)).astype(x.dtype)

def rotary(x, positions):
    half = HEAD_DIM // 2
    inv_freq = ROPE_BASE ** (-jnp.arange(half, dtype=jnp.float32) / half)
    ang = positions.astype(jnp.float32)[..., None] * inv_freq
    cos = jnp.cos(ang)[:, :, None, :]
    sin = jnp.sin(ang)[:, :, None, :]
    x1 = x[..., :half].astype(jnp.float32)
    x2 = x[..., half:].astype(jnp.float32)
    out = jnp.concatenate([x1 * cos - x2 * sin, x2 * cos + x1 * sin], axis=-1)
    return out.astype(x.dtype)

def retention(q, k, v, positions):
    B, S, H, D = q.shape
    C = RET_CHUNK
    NC = S // C
    q = rotary(q, positions)
    k = rotary(k, positions) * (D ** -0.5)
    log_g = jnp.log1p(-(2.0 ** (-5.0 - jnp.arange(H, dtype=jnp.float32))))
    idx = jnp.arange(C, dtype=jnp.float32)
    rel = idx[:, None] - idx[None, :]
    decay_intra = jnp.where(rel >= 0, jnp.exp(log_g[:, None, None] * jnp.maximum(rel, 0.0)), 0.0)
    xi = jnp.exp(log_g[:, None] * (idx + 1.0))
    zeta = jnp.exp(log_g[:, None] * (C - 1.0 - idx))
    chunk_decay = jnp.exp(log_g * C)
    qc = q.reshape(B, NC, C, H, D)
    kc = k.reshape(B, NC, C, H, D)
    vc = v.reshape(B, NC, C, H, D)
    scores = jnp.einsum('bnihd,bnjhd->bnhij', qc, kc) * decay_intra
    y_intra = jnp.einsum('bnhij,bnjhd->bnihd', scores, vc)
    kv = jnp.einsum('bnjhd,hj,bnjhe->nbhde', kc, zeta, vc).astype(jnp.float32)

    def step(state, kv_i):
        return chunk_decay[None, :, None, None] * state + kv_i, state

    _, states = lax.scan(step, jnp.zeros((B, H, D, D), jnp.float32), kv)
    y_cross = jnp.einsum('bnihd,nbhde,hi->bnihe', qc, states, xi)
    return (y_intra + y_cross).reshape(B, S, H, D)

def head_group_norm(y, gain):
    B, S, H, D = y.shape
    yf = y.astype(jnp.float32)
    mu = jnp.mean(yf, axis=-1, keepdims=True)
    var = jnp.mean(jnp.square(yf - mu), axis=-1, keepdims=True)
    yn = (yf - mu) * lax.rsqrt(var + EPS)
    return yn.reshape(B, S, H * D) * gain.astype(jnp.float32)

def stick_breaking(q, k, v):
    B, S, H, D = q.shape
    NB = S // SB_BLOCK
    q_blocks = q.reshape(B, NB, SB_BLOCK, H, D).transpose(1, 0, 3, 2, 4)
    kt = k.transpose(0, 2, 1, 3)
    vt = v.transpose(0, 2, 1, 3)
    key_pos = jnp.arange(S)
    scale = D ** -0.5

    def block(args):
        qi, start = args
        z = jnp.einsum('bhqd,bhsd->bhqs', qi, kt).astype(jnp.float32) * scale
        q_pos = start + jnp.arange(SB_BLOCK)
        mask = key_pos[None, :] < q_pos[:, None]
        log_beta = jax.nn.log_sigmoid(z)
        log_stay = jnp.where(mask, log_beta - z, 0.0)
        log_w = log_beta + lax.cumsum(log_stay, axis=3, reverse=True) - log_stay
        w = jnp.where(mask, jnp.exp(log_w), 0.0)
        return jnp.einsum('bhqs,bhsd->bhqd', w.astype(vt.dtype), vt)

    starts = jnp.arange(NB) * SB_BLOCK
    out = lax.map(block, (q_blocks, starts))
    return out.transpose(1, 0, 3, 2, 4).reshape(B, S, H, D)

def peer(h, w_query, sub_keys, expert_down, expert_up):
    B, S, Dm = h.shape
    T = B * S
    K = PEER_TOPK
    ht = h.reshape(T, Dm)
    qry = (ht @ w_query).reshape(T, PEER_HEADS, 2, PEER_HALF_2)
    sub_scores = jnp.einsum('thpc,hpkc->thpk', qry, sub_keys).astype(jnp.float32)
    top_s, top_i = lax.top_k(sub_scores, K)
    cand_s = top_s[:, :, 0, :, None] + top_s[:, :, 1, None, :]
    cand_id = top_i[:, :, 0, :, None] * N_KEYS + top_i[:, :, 1, None, :]
    best_s, best_c = lax.top_k(cand_s.reshape(T, PEER_HEADS, K * K), K)
    expert_id = jnp.take_along_axis(cand_id.reshape(T, PEER_HEADS, K * K), best_c, axis=-1)
    gate = jax.nn.softmax(best_s, axis=-1)
    NBK = T // PEER_BLOCK
    ids = expert_id.reshape(NBK, PEER_BLOCK, PEER_HEADS * K)
    gates = gate.reshape(NBK, PEER_BLOCK, PEER_HEADS * K)
    xs = ht.reshape(NBK, PEER_BLOCK, Dm)

    def block(args):
        xb, ib, gb = args
        u = expert_down[ib]
        a = jnp.einsum('pd,ped->pe', xb, u).astype(jnp.float32)
        act = jax.nn.gelu(a, approximate=False) * gb
        v = expert_up[ib]
        return jnp.einsum('pe,ped->pd', act.astype(xb.dtype), v)

    y = lax.map(block, (xs, ids, gates))
    return y.reshape(B, S, Dm)

def second_inputs(seed: int = 0) -> dict:
    key = jax.random.key(seed)
    ks = jax.random.split(key, 16)
    f32 = jnp.float32
    nrm = lambda k, shape, s: jax.random.normal(k, shape, f32) * s
    return {
        "x": nrm(ks[0], (BATCH, SEQ, D_MODEL), 1.0),
        "c": nrm(ks[1], (BATCH, D_MODEL), 1.0),
        "positions": jnp.broadcast_to(jnp.arange(SEQ, dtype=jnp.int32)[None, :], (BATCH, SEQ)),
        "ada_w": nrm(ks[2], (DEPTH, D_MODEL, 6 * D_MODEL), D_MODEL ** -0.5),
        "ada_b": nrm(ks[3], (DEPTH, 6 * D_MODEL), 0.1),
        "norm1_gain": 1.0 + nrm(ks[4], (DEPTH, D_MODEL), 0.1),
        "norm2_gain": 1.0 + nrm(ks[5], (DEPTH, D_MODEL), 0.1),
        "w_in": nrm(ks[6], (DEPTH, D_MODEL, IN_COLS), D_MODEL ** -0.5),
        "ret_norm_gain": 1.0 + nrm(ks[7], (DEPTH, RET_WIDTH), 0.1),
        "sb_q_gain": 1.0 + nrm(ks[8], (DEPTH, HEAD_DIM), 0.1),
        "sb_k_gain": 1.0 + nrm(ks[9], (DEPTH, HEAD_DIM), 0.1),
        "sb_out_gain": 1.0 + nrm(ks[10], (DEPTH, HEAD_DIM), 0.1),
        "w_out": nrm(ks[11], (DEPTH, D_MIX, D_MODEL), D_MIX ** -0.5),
        "peer_w_query": nrm(ks[12], (DEPTH, D_MODEL, PEER_HEADS * PEER_QDIM), D_MODEL ** -0.5),
        "peer_sub_keys": nrm(ks[13], (DEPTH, PEER_HEADS, 2, N_KEYS, PEER_HALF_2), PEER_HALF_2 ** -0.5),
        "peer_down": nrm(ks[14], (DEPTH, N_EXPERTS, D_MODEL), D_MODEL ** -0.5),
        "peer_up": nrm(ks[15], (DEPTH, N_EXPERTS, D_MODEL), PEER_HEADS ** -0.5),
    }

def second_block(x, c, positions, ada_w, ada_b, norm1_gain, norm2_gain, w_in, ret_norm_gain,
              sb_q_gain, sb_k_gain, sb_out_gain, w_out, peer_w_query, peer_sub_keys,
              peer_down, peer_up):
    B, S, _ = x.shape
    for layer in range(DEPTH):
        mod = jax.nn.silu(c) @ ada_w[layer] + ada_b[layer]
        shift1, scale1, gate1, shift2, scale2, gate2 = jnp.split(mod[:, None, :], 6, axis=-1)

        h = rms_norm_2(x, norm1_gain[layer]) * (1.0 + scale1) + shift1
        proj = h @ w_in[layer]
        r_q, r_k, r_v, r_g, s_q, s_k, s_v = jnp.split(
            proj, np.cumsum([RET_WIDTH] * 4 + [SB_WIDTH] * 2), axis=-1)
        heads_r = lambda t: t.reshape(B, S, N_RET_HEADS, HEAD_DIM)
        heads_s = lambda t: t.reshape(B, S, N_SB_HEADS, HEAD_DIM)

        y_ret = retention(heads_r(r_q), heads_r(r_k), heads_r(r_v), positions)
        y_ret = head_group_norm(y_ret, ret_norm_gain[layer]) * jax.nn.silu(r_g.astype(jnp.float32))

        q_sb = rms_norm_2(heads_s(s_q), sb_q_gain[layer])
        k_sb = rms_norm_2(heads_s(s_k), sb_k_gain[layer])
        y_sb = stick_breaking(q_sb, k_sb, heads_s(s_v))
        y_sb = rms_norm_2(y_sb, sb_out_gain[layer]).reshape(B, S, SB_WIDTH)

        mixed = jnp.concatenate([y_ret.astype(x.dtype), y_sb.astype(x.dtype)], axis=-1) @ w_out[layer]
        x = x + gate1 * mixed

        h2 = rms_norm_2(x, norm2_gain[layer]) * (1.0 + scale2) + shift2
        ffn = peer(h2, peer_w_query[layer], peer_sub_keys[layer], peer_down[layer], peer_up[layer])
        x = x + gate2 * ffn
    return x


def setup_inputs(seed=0):
    out = dict(first_inputs(seed))
    for name, value in second_inputs(seed + 1).items():
        if name != "x":
            out[name + "_2"] = value
    return out


def reference(
    x, norm1_g, w_in, hg_lower_logits, hg_norm_g, gla_w_gate_up, gla_b_gate, gla_norm_g, w_out,
    norm2_g, peer_w_q, peer_sub_keys, peer_u, peer_v, norm_f_g, c_2, positions_2, ada_w_2,
    ada_b_2, norm1_gain_2, norm2_gain_2, w_in_2, ret_norm_gain_2, sb_q_gain_2, sb_k_gain_2,
    sb_out_gain_2, w_out_2, peer_w_query_2, peer_sub_keys_2, peer_down_2, peer_up_2,
):
    x = first_block(
        x, norm1_g, w_in, hg_lower_logits, hg_norm_g, gla_w_gate_up, gla_b_gate, gla_norm_g,
        w_out, norm2_g, peer_w_q, peer_sub_keys, peer_u, peer_v, norm_f_g,
    )
    return second_block(
        x, c_2, positions_2, ada_w_2, ada_b_2, norm1_gain_2, norm2_gain_2, w_in_2,
        ret_norm_gain_2, sb_q_gain_2, sb_k_gain_2, sb_out_gain_2, w_out_2, peer_w_query_2,
        peer_sub_keys_2, peer_down_2, peer_up_2,
    )


_drawn_inputs = setup_inputs


def setup_inputs(seed=0):
    import zlib

    import numpy as np

    out = dict(_drawn_inputs(seed))
    spreads = {}
    factors = {'hg_lower_logits': 3.486,
     'hg_norm_g': 2.736,
     'sb_q_gain_2': 2.977,
     'sb_k_gain_2': 3.081,
     'gla_norm_g': 3.164,
     'norm2_g': 2.691}
    for name, (base, spread) in spreads.items():
        noise = np.random.default_rng([zlib.crc32(name.encode()), seed]).standard_normal(out[name].shape)
        drawn = base * np.exp(spread * noise) if base else spread * noise
        out[name] = __import__('jax').numpy.asarray(drawn.astype(out[name].dtype))
    for name, factor in factors.items():
        out[name] = (out[name] * factor).astype(out[name].dtype)
    return out
```

```python
from contextlib import ExitStack

import numpy as np

import concourse.bass as bass
from concourse import mybir

F32 = mybir.dt.float32
U32 = mybir.dt.uint32
I32 = mybir.dt.int32
ALU = mybir.AluOpType
ACT = mybir.ActivationFunctionType
AX_X = mybir.AxisListType.X

P = 128
D = 1024
KC = D // P
SEQ = 512
NT = SEQ // P
SEC = 512
CHUNK = 64
NCH = SEQ // CHUNK
EPS = 1e-6
NH, TOPK, NKEY = 8, 16, 128
SLOTS = NH * TOPK
RING = 8
GROUPS = SLOTS // RING
IN_TILE = (64, 32, 16, 8, 4, 2, 1)
NLEV = len(IN_TILE) + 1
NEG = -3.0e38
TWO_PI = 6.283185307179586
ROUND = 12582912.0


def constants():
    j, i = np.meshgrid(np.arange(P), np.arange(P), indexing="ij")
    levels = [((j // s) % 2 == 0) & (i // s == j // s + 1) for s in IN_TILE] + [i == j]
    rel = np.arange(SEQ)[None, :] - np.arange(P)[:, None]
    gamma = 1.0 - 2.0 ** (-5.0 - np.arange(8))
    decay = np.where(rel >= 0, gamma[:, None, None] ** np.maximum(rel, 0), 0.0) * 64 ** -0.5
    split = 6.28125
    rest = float(np.float32(TWO_PI - split))
    return {
        "c_ident": np.eye(P, dtype=np.float32),
        "c_levels": np.stack(levels, 1).astype(np.float32).reshape(P, NLEV * P),
        "c_reset": np.broadcast_to((np.arange(SEQ) % CHUNK != 0).astype(np.float32), (P, SEQ)).copy(),
        "c_sticks": np.stack([-(j >= i).astype(np.float32), -np.ones((P, P), np.float32),
                              (j < i).astype(np.float32)], 1).reshape(P, 3 * P),
        "c_decay": decay.astype(np.float32),
        "c_freq": np.broadcast_to((10000.0 ** (-np.arange(32) / 32)).astype(np.float32), (P, 32)).copy(),
        "c_iota": np.broadcast_to(np.arange(16, dtype=np.float32), (P, 16)).copy(),
    }, (split, rest, float(np.float32(TWO_PI - split - rest)))


class Chain:

    def __init__(self, eng, sem):
        self.eng, self.sem, self.n = eng, sem, 0

    def restart(self):
        self.eng.sem_clear(self.sem)
        self.n = 0

    def __call__(self, ins):
        self.n += 1
        ins.then_inc(self.sem, 1)
        self.eng.wait_ge(self.sem, self.n)


class Seen:

    def __init__(self, eng):
        self.eng, self.n = eng, {}

    def next(self, sem, by=1):
        self.n[sem.name] = self.n.get(sem.name, 0) + by
        self.eng.wait_ge(sem, self.n[sem.name])


def build(nc, a, out, two_pi):
    with ExitStack() as ctx:
        def sb(name, cols, dt=F32):
            return ctx.enter_context(nc.sbuf_tensor(name, [P, cols], dt))[:, :]

        def sem(name):
            return ctx.enter_context(nc.semaphore(name))

        psum = ctx.enter_context(nc.psum_tensor("psum", [P, 8 * 512], F32))[:, :]
        ps = [psum[:, n * 512:(n + 1) * 512] for n in range(8)]

        x = sb("x", NT * D).rearrange("p (t d) -> p t d", t=NT)
        hn = sb("hn", NT * D).rearrange("p (t d) -> p t d", t=NT)
        hT_ = sb("hT", NT * D)
        hT = hT_.rearrange("p (k n) -> p k n", k=KC)
        w_ = sb("w", 2 * KC * SEC)
        wsec = [w_[:, s * KC * SEC:(s + 1) * KC * SEC].rearrange("p (k n) -> p k n", k=KC) for s in range(2)]
        big = sb("big", 64 * 256)
        modm = sb("mod", 6 * D)
        mod = modm.rearrange("p (r d) -> p r d", r=6)
        rows = sb("rows", 3 * D).rearrange("p (r d) -> p r d", r=3)
        tmp = sb("tmp", 12 * 256)
        srow = sb("srow", 1024)
        lev_ = sb("levels", NLEV * P)
        ident = sb("ident", P)
        small = sb("small", 256)

        def part(base, at_kib, kib, dt=F32):
            v = base[:, int(at_kib * 256):int((at_kib + kib) * 256)]
            return v if dt == F32 else v.bitcast(dt)

        qT = part(big, 0, 12).rearrange("p (g n) -> p g n", g=6)
        kT = part(big, 12, 12).rearrange("p (g n) -> p g n", g=6)
        cum = part(big, 24, 12).rearrange("p (g n) -> p g n", g=6)
        v1 = part(big, 36, 16).rearrange("p (m t n) -> p m t n", m=2, t=NT)
        sg1 = modm[:, 0:4096].rearrange("p (m t n) -> p m t n", m=2, t=NT)
        NQK = len(IN_TILE) + 2
        qk = [part(big, 52 + 2 * n, 2) for n in range(6)] + [modm[:, 4096 + 512 * n:4608 + 512 * n] for n in range(3)]
        st1 = [hT_[:, b * 2048:(b + 1) * 2048].rearrange("p (j n) -> p j n", j=NT) for b in range(2)]
        ex = [part(tmp, 2 * n, 2) for n in range(3)]
        mk = part(tmp, 6, 4)
        reset = part(tmp, 10, 2)
        glow = srow[0:16, 512:1024]
        w_low = rows[:, 2, 0:KC * 16].rearrange("p (k n) -> p k n", k=KC)
        w_up = rows[0:16, 2, 256:512]
        tot = part(small, 0, 0.1875)
        offs = part(rows[:, 2, :], 2, 0.5625).rearrange("p (l g c) -> p l g c", l=3, g=6)
        levels = lev_
        s_all = part(big, 0, 32)
        keysT = part(big, 32, 8).rearrange("p (m n) -> p m n", m=16)
        qst = [part(big, 40 + 2 * b, 2) for b in range(2)]
        stage = part(big, 44, 8).rearrange("p (m n) -> p m n", m=16)
        onehot = part(big, 52, 8)
        cand = part(big, 60, 1)
        tv = part(big, 61, 1).rearrange("p (h s k) -> p h s k", h=NH, s=2)
        tif = part(big, 62, 1).rearrange("p (h s k) -> p h s k", h=NH, s=2)
        ti = part(big, 63, 1, U32).rearrange("p (h s k) -> p h s k", h=NH, s=2)
        ur = [part(big, 4 * b, 4) for b in range(RING)]
        vr = [part(big, 32 + 4 * b, 4) for b in range(RING)]
        y = part(tmp, 0, 4)
        bv = part(tmp, 0, 0.5).rearrange("p (h k) -> p h k", h=NH)
        bp = part(tmp, 0.5, 0.5, U32).rearrange("p (h k) -> p h k", h=NH)
        pai = part(tmp, 1, 0.5, U32)
        paf = part(tmp, 1.5, 0.5)
        ia = part(tmp, 2, 0.5)
        ib = part(tmp, 2.5, 0.5)
        idf = part(tmp, 3, 0.5)
        idx = part(tmp, 4, 2, U32)
        gate = part(tmp, 6, 2)
        crep = part(tmp, 8, 4).rearrange("p (k n) -> p k n", k=KC)
        rqT, rkT, sqT, skT = [part(big, 8 * n, 8).rearrange("p (g n) -> p g n", g=4) for n in range(4)]
        rv = part(big, 32, 8).rearrange("p (t n) -> p t n", t=NT)
        sv = part(big, 40, 8).rearrange("p (t n) -> p t n", t=NT)
        rg = part(big, 48, 8).rearrange("p (t n) -> p t n", t=NT)
        dec = [part(big, 56 + 2 * b, 2) for b in range(2)]
        sin = part(big, 60, 0.5).rearrange("p (t n) -> p t n", t=NT)
        nsin = part(big, 60.5, 0.5).rearrange("p (t n) -> p t n", t=NT)
        cos = part(big, 61, 0.5).rearrange("p (t n) -> p t n", t=NT)
        ang = part(big, 61.5, 0.5).rearrange("p (t n) -> p t n", t=NT)
        turn = part(big, 62, 0.5).rearrange("p (t n) -> p t n", t=NT)
        rt = [part(tmp, 2 * n, 2) for n in range(2)]
        sq = part(tmp, 4, 2)
        t3 = part(tmp, 6, 2)
        ab = [part(tmp, 2 * n, 2) for n in range(2)]
        stay = [part(big, 8 * n, 8).rearrange("p (j n) -> p j n", j=NT) for n in range(2)]
        scr = part(tmp, 8, 4)
        pos = small[:, 200:204].bitcast(I32)
        posf = small[:, 204:208]
        freq = small[:, 208:240]
        iota = small[:, 240:256]
        ss = small[:, 0:32]
        var = small[:, 32:64]
        std = small[:, 64:96]
        rs = small[:, 96:128]
        nt_ = small[:, 128:160]
        a8 = small[:, 160:168]
        g8 = small[:, 168:176]
        c8 = small[:, 176:184]
        i8 = [small[:, 184 + 8 * b:192 + 8 * b].bitcast(U32) for b in range(2)]
        ccol = sb("ccol", 64)
        lb = sb("lb", 64)
        lb3 = lb[:, 0:24].rearrange("p (r h) -> p r h", r=6)
        bg = lb[:, 32:34]
        sticks = lev_[:, 0:3 * P].rearrange("p (m n) -> p m n", m=3)
        arow = lev_[0:1, 512:1024]
        ones = sb("ones", P)

        c_top, c_dve, c_act, c_pool = sem("choice_step"), sem("dve_step"), sem("act_step"), sem("pool_step")
        x_in = sem("x_landed")
        cst_in = sem("constants_landed")
        keys_in = sem("keys_landed")
        row_in = sem("rows_landed")
        w_landed = [sem(f"w_landed{s}") for s in range(2)]
        dec_in = [sem(f"decay_landed{s}") for s in range(2)]
        ada_row_in = sem("ada_b_landed")
        pj_done = sem("projected")
        pj_free = [sem(f"projection_read{b}") for b in range(2)]
        tr_done = sem("transposed")
        tr_free = [sem(f"transposed_read{b}") for b in range(2)]
        src_ready = sem("to_transpose")
        ss_done = sem("squares_ready")
        var_ready = sem("variance_ready")
        std_ready = sem("deviation_ready")
        act_to_dve = sem("act_to_dve")
        dve_to_act = sem("dve_to_act")
        x_ready = sem("x_ready")
        ex_sub = sem("exponents_ready")
        ex_done = sem("exponentials_ready")
        qk_ready = sem("decayed_ready")
        lev_done = sem("levels_scored")
        lev_used = sem("levels_masked")
        st_ready = sem("near_scores_ready")
        far_done = sem("far_scored")
        far_copied = sem("far_copied")
        pv_done = sem("values_summed")
        pv_used = sem("values_read")
        low_done = sem("low_rank_done")
        low_copied = sem("low_rank_copied")
        low_used = sem("low_rank_read")
        sc_done = sem("keys_scored")
        sc_used = sem("key_scores_copied")
        top_ready = sem("experts_chosen")
        u_in = [sem(f"u_landed{b}") for b in range(RING)]
        v_in = [sem(f"v_landed{b}") for b in range(RING)]
        u_free, v_free = sem("u_slots_free"), sem("v_slots_free")
        act_in, act_out, c8_ready = sem("gelu_wanted"), sem("gelu_ready"), sem("weights_of_group_ready")
        crep_ready = sem("c_spread")
        z_done = sem("sticks_scored")
        z_used = sem("sticks_read")
        ln_ready = sem("softplus_ready")
        sp_ready = sem("stays_ready")
        ar_done = sem("stick_logs_summed")
        w_exp = sem("weights_raised")
        wt_ready = sem("weights_ready")
        out_ready = sem("out_ready")
        out_done = sem("out_stored")

        def cols(w, k):
            return [(w, s * SEC) for s in range(k)]

        w_in1 = a["w_in"]
        order = [(w_in1, 0), (w_in1, 512), (w_in1, 1024), (w_in1, 1536), (w_in1, 2048), (w_in1, 2560), (w_in1, 3088)]
        order += cols(a["w_out"], 2) + cols(a["peer_w_q"], 4) + cols(a["ada_w_2"], 12)
        order += cols(a["w_in_2"], 7) + cols(a["w_out_2"], 2) + cols(a["peer_w_query_2"], 4)
        outputs = [1 if w is a["ada_w_2"] else 4 for w, _ in order]
        before = [sum(outputs[:n]) for n in range(len(order) + 1)]

        layer_u = [a["peer_u"], a["peer_down_2"]]
        layer_v = [a["peer_v"], a["peer_up_2"]]
        layer_keys = [a["keysT"], a["keysT_2"]]
        block = ctx.enter_context(nc.Block())

        @block.sync
        def _(sp):
            def load_section(n):
                w, at = order[n]
                if n >= 2:
                    sp.wait_ge(pj_done, before[n - 1])
                sp.dma_start(wsec[n % 2], w[:, at:at + SEC].rearrange("(k p) n -> p k n", p=P)).then_inc(w_landed[n % 2], 16)

            for t in range(NT):
                sp.dma_start(x[:, t, :], a["x"][t * P:(t + 1) * P, :]).then_inc(x_in, 16)
            sp.dma_start(rows[:, 0, :], a["norm1_g"].partition_broadcast(P)).then_inc(row_in, 16)
            sp.dma_start(ident, a["c_ident"]).then_inc(cst_in, 16)
            sp.dma_start(levels, a["c_levels"]).then_inc(cst_in, 16)
            sp.dma_start(reset, a["c_reset"]).then_inc(cst_in, 16)
            sp.dma_start(iota, a["c_iota"]).then_inc(cst_in, 16)
            sp.dma_start(freq, a["c_freq"]).then_inc(cst_in, 16)
            sp.dma_start(w_low, a["w_in"][:, 3072:3088].rearrange("(k p) n -> p k n", p=P)).then_inc(cst_in, 16)
            sp.dma_start(w_up, a["gla_w_gate_up"]).then_inc(cst_in, 16)
            with nc.allow_non_contiguous_dma(reason="a few hundred values, one to a partition"):
                sp.dma_start(lb3[:, 0:2, :], a["hg_lower_logits"].rearrange("r (h p) -> p r h", p=P)).then_inc(cst_in, 16)
                sp.dma_start(bg, a["gla_b_gate"].rearrange("(h p) -> p h", p=P)).then_inc(cst_in, 16)
                sp.dma_start(ccol[:, 0:KC], a["c_2"].rearrange("(k p) -> p k", p=P)).then_inc(cst_in, 16)
                sp.dma_start(pos, a["positions_2"].rearrange("(t p) -> p t", p=P)).then_inc(cst_in, 16)
            sp.dma_start(srow[:, 0:128], a["hg_norm_g"].partition_broadcast(P)).then_inc(cst_in, 16)
            sp.dma_start(srow[:, 128:256], a["gla_norm_g"].partition_broadcast(P)).then_inc(cst_in, 16)
            sp.dma_start(rows[:, 1, :], a["norm2_g"].partition_broadcast(P)).then_inc(row_in, 16)
            for n in range(9):
                load_section(n)
            sp.wait_ge(pv_used, 8)
            sp.dma_start(keysT, layer_keys[0].rearrange("d (m n) -> d m n", m=16)).then_inc(keys_in, 16)
            sp.dma_start(rows[:, 2, :], a["norm_f_g"].partition_broadcast(P)).then_inc(keys_in, 16)
            for n in range(9, 13):
                load_section(n)
            for n in range(13, 25):
                load_section(n)
                if n > 13:
                    sp.wait_ge(pj_done, before[n])
                sp.dma_start(arow, a["ada_b_2"][None, (n - 13) * SEC:(n - 12) * SEC]).then_inc(ada_row_in, 16)
            load_section(25)
            sp.wait_ge(src_ready, 3 * NT)
            sp.dma_start(rows[:, 0, :], a["norm1_gain_2"].partition_broadcast(P)).then_inc(row_in, 16)
            sp.dma_start(rows[:, 1, :], a["norm2_gain_2"].partition_broadcast(P)).then_inc(row_in, 16)
            sp.dma_start(srow[:, 0:512], a["ret_norm_gain_2"].partition_broadcast(P)).then_inc(row_in, 16)
            sp.dma_start(srow[:, 512:576], a["sb_q_gain_2"].partition_broadcast(P)).then_inc(row_in, 16)
            sp.dma_start(srow[:, 576:640], a["sb_k_gain_2"].partition_broadcast(P)).then_inc(row_in, 16)
            sp.dma_start(srow[:, 640:704], a["sb_out_gain_2"].partition_broadcast(P)).then_inc(row_in, 16)
            sp.wait_ge(pj_done, before[25])
            sp.dma_start(lev_[:, 0:3 * P], a["c_sticks"]).then_inc(row_in, 16)
            for n in range(26, 32):
                load_section(n)
            for h in range(8):
                if h >= 2:
                    sp.wait_ge(wt_ready, NT * (h - 1))
                else:
                    sp.wait_ge(v_free, RING + NT * SLOTS)
                sp.dma_start(dec[h % 2], a["c_decay"][h]).then_inc(dec_in[h % 2], 16)
            load_section(32)
            load_section(33)
            sp.wait_ge(pv_used, 8 + 16)
            sp.dma_start(keysT, layer_keys[1].rearrange("d (m n) -> d m n", m=16)).then_inc(keys_in, 16)
            for n in range(34, 38):
                load_section(n)
            for t in range(NT):
                sp.wait_ge(out_ready, t + 1)
                sp.dma_start(out[t * P:(t + 1) * P, :], x[:, t, :]).then_inc(out_done, 16)
            sp.wait_ge(out_done, 16 * NT)

        @block.tensor
        def _(pe):
            seen = Seen(pe)
            n_out, n_tr, n_sec = [0], [0], [0]

            def next_bank():
                n = n_out[0]
                n_out[0] += 1
                if n >= 2:
                    pe.wait_ge(pj_free[n % 2], n // 2)
                return ps[n % 2]

            def section():
                n = n_sec[0]
                n_sec[0] += 1
                pe.wait_ge(w_landed[n % 2], 16 * (n // 2 + 1))
                return wsec[n % 2]

            def project_tokens():
                w = section()
                for t in range(NT):
                    bank = next_bank()
                    for k in range(KC):
                        last = nc.tensor.matmul(bank, hT[:, k, t * P:(t + 1) * P], w[:, k, :], start=k == 0, stop=k == KC - 1)
                    last.then_inc(pj_done, 1)

            def project_columns():
                w = section()
                for c in range(SEC // P):
                    bank = next_bank()
                    for k in range(KC):
                        last = nc.tensor.matmul(bank, w[:, k, c * P:(c + 1) * P], hT[:, k, :], start=k == 0, stop=k == KC - 1)
                    last.then_inc(pj_done, 1)

            def transpose4(blocks):
                n = n_tr[0]
                n_tr[0] += 1
                if n >= 2:
                    pe.wait_ge(tr_free[n % 2], n // 2)
                for b, s in enumerate(blocks):
                    last = nc.tensor.transpose(ps[2 + n % 2][:, b * P:(b + 1) * P], s, ident)
                last.then_inc(tr_done, 1)

            def transposes_read():
                for b in range(2):
                    pe.wait_ge(tr_free[b], n_tr[0] // 2)

            def transpose_tokens():
                for t in range(NT):
                    seen.next(src_ready)
                    for b in range(2):
                        transpose4([hn[:, t, (4 * b + c) * P:(4 * b + c + 1) * P] for c in range(4)])
                transposes_read()

            def queries(layer):
                pe.wait_ge(keys_in, 16 * (2 + layer))

                def scores_of(m):
                    n = n_out[0] - 1 if m < 15 else n_out[0]
                    n -= 1
                    pe.wait_ge(pj_free[n % 2], n // 2 + 1)
                    if m >= 2:
                        pe.wait_ge(sc_used, 16 * layer + m - 1)
                    for t in range(NT):
                        last = nc.tensor.matmul(ps[4 + m % 2][:, t * P:(t + 1) * P], qst[m % 2][:, t * P:(t + 1) * P],
                                                keysT[:, m, :], start=True, stop=True)
                    last.then_inc(sc_done, 1)

                for s in range(4):
                    w = section()
                    for c in range(4):
                        bank = next_bank()
                        for k in range(KC):
                            last = nc.tensor.matmul(bank, w[:, k, c * P:(c + 1) * P], hT[:, k, :],
                                                    start=k == 0, stop=k == KC - 1)
                        last.then_inc(pj_done, 1)
                        if 4 * s + c:
                            scores_of(4 * s + c - 1)
                scores_of(15)

            seen.next(cst_in, 16 * 13)
            transpose_tokens()
            project_columns()
            project_columns()
            project_tokens()
            project_tokens()
            project_columns()
            for k in range(KC):
                last = nc.tensor.matmul(ps[4][0:16, :], w_low[:, k, :], hT[:, k, :], start=k == 0, stop=k == KC - 1)
            last.then_inc(low_done, 1)
            project_tokens()
            seen.next(low_copied)
            for c in range(2):
                last = nc.tensor.matmul(ps[5 + c], w_up[:, c * P:(c + 1) * P], glow, start=True, stop=True)
            last.then_inc(low_done, 1)
            project_tokens()

            def mix1(g, h, prt):
                if h >= 1:
                    pe.wait_ge(far_copied, h)
                q256, q128 = qk[0][prt], qk[1][prt]
                nc.tensor.matmul(ps[2][:, 0:256], q256[:, 0:P], q256[:, 256:512], start=True, stop=True)
                nc.tensor.matmul(ps[2][:, 256:512], q256[:, P:2 * P], q256[:, 256:512], start=True, stop=True)
                nc.tensor.matmul(ps[3][:, 0:P], q128[:, 0:P], q128[:, P:2 * P], start=True, stop=True)
                nc.tensor.matmul(ps[3][:, P:2 * P], q128[:, 2 * P:3 * P], q128[:, 3 * P:4 * P], start=True, stop=True)\
                    .then_inc(far_done, 1)
                for t in range(NT):
                    n = h * NT + t
                    if n >= 2:
                        pe.wait_ge(lev_used, n - 1)
                    tt = slice(t * P, (t + 1) * P)
                    for l in range(NLEV):
                        lhs, rhs = (qk[2 + l], qk[2 + l]) if l < NLEV - 1 else (kT[:, g, :], qT[:, g, :])
                        last = nc.tensor.matmul(ps[4 + 2 * (n % 2) + l // 4][:, (l % 4) * P:(l % 4 + 1) * P],
                                                lhs[prt][:, tt], rhs[prt][:, tt], start=True, stop=True)
                    last.then_inc(lev_done, 1)

            def values(h, st, v_of, width, first=False):
                if not first:
                    seen.next(pv_used)
                for t in range(NT):
                    for j in range(t + 1):
                        last = nc.tensor.matmul(ps[0][:, t * width:(t + 1) * width], st[:, j, t * P:(t + 1) * P], v_of(j),
                                                start=j == 0, stop=j == t)
                last.then_inc(pv_done, 1)

            def values1(h):
                pe.wait_ge(st_ready, (h + 1) * NT)
                pe.wait_ge(far_copied, h + 1)
                m, c = (0, h) if h < 4 else (1, h - 4)
                values(h, st1[h % 2], lambda j: v1[:, m, j, c * P:(c + 1) * P], P, first=h == 0)

            full, heads = slice(0, P), [slice(0, 64), slice(64, P)]
            of_group = [(g, full) for g in range(4)] + [(4 + n // 2, heads[n % 2]) for n in range(4)]
            pe.wait_ge(pj_free[0], (n_out[0] + 1) // 2)
            for h, (g, prt) in enumerate(of_group):
                if h < 4 or h % 2 == 0:
                    seen.next(qk_ready, NQK)
                mix1(g, h, prt)
                if h >= 1:
                    values1(h - 1)
            values1(7)
            seen.next(pv_used)
            transpose_tokens()
            project_tokens()
            project_tokens()
            transpose_tokens()
            queries(0)
            seen.next(crep_ready)
            for n in range(12):
                w = section()
                bank = next_bank()
                for k in range(KC):
                    nc.tensor.matmul(bank, crep[:, k, :], w[:, k, :], start=k == 0, stop=False)
                seen.next(ada_row_in, 16)
                nc.tensor.matmul(bank, ones[0:1, :], arow, start=False, stop=True).then_inc(pj_done, 1)

            transpose_tokens()

            def project_and_turn():
                w = section()
                for t in range(NT):
                    bank = next_bank()
                    for k in range(KC):
                        last = nc.tensor.matmul(bank, hT[:, k, t * P:(t + 1) * P], w[:, k, :], start=k == 0, stop=k == KC - 1)
                    last.then_inc(pj_done, 1)
                    if t:
                        turn_one()
                turn_one()

            n_turn = [0]

            def turn_one():
                r = rt[n_turn[0] % 2]
                n_turn[0] += 1
                seen.next(src_ready)
                transpose4([r[:, c * P:(c + 1) * P] for c in range(4)])

            project_and_turn()
            project_and_turn()
            project_tokens()
            project_tokens()
            project_and_turn()
            project_and_turn()
            project_tokens()
            transposes_read()
            pe.wait_ge(pj_free[0], (n_out[0] + 1) // 2)
            pe.wait_ge(pj_free[1], n_out[0] // 2)
            for h in range(8):
                prt = heads[h % 2]
                for j in range(NT):
                    n = h * NT + j
                    if n >= 4:
                        pe.wait_ge(wt_ready, n - 3)
                    nc.tensor.matmul(ps[4 + n % 4][:, 0:SEQ - j * P], rkT[prt, h // 2, j * P:(j + 1) * P],
                                     rqT[prt, h // 2, j * P:SEQ], start=True, stop=True).then_inc(z_done, 1)
                if h >= 1:
                    pe.wait_ge(wt_ready, h * NT)
                    values(h - 1, st1[(h - 1) % 2], lambda j: rv[:, j, (h - 1) * 64:h * 64], 64, first=h == 1)
            pe.wait_ge(wt_ready, 8 * NT)
            values(7, st1[1], lambda j: rv[:, j, 448:512], 64)

            def score(h, j, bank, start, stop):
                prt = heads[h % 2]
                return nc.tensor.matmul(bank[:, 0:SEQ - j * P], skT[prt, h // 2, j * P:(j + 1) * P],
                                        sqT[prt, h // 2, j * P:SEQ], start=start, stop=stop)

            for n in range(8 * NT + 1):
                h, j = n // NT, NT - 1 - n % NT
                if n < 8 * NT:
                    if n >= 2:
                        pe.wait_ge(z_used, n - 1)
                    score(h, j, ps[4 + n % 2], True, True).then_inc(z_done, 1)
                if n >= 1:
                    m = n - 1
                    h, j = m // NT, NT - 1 - m % NT
                    pe.wait_ge(sp_ready, m + 1)
                    if m >= 2:
                        pe.wait_ge(wt_ready, 8 * NT + m - 1)
                    bank = ps[6 + m % 2]
                    score(h, j, bank, True, False)
                    for i in range(NT - 1, j - 1, -1):
                        last = nc.tensor.matmul(bank[:, (i - j) * P:SEQ - j * P], sticks[:, 0 if i == j else 1, :],
                                                stay[h % 2][:, i, i * P:SEQ], start=False, stop=i == j)
                    last.then_inc(ar_done, 1)
                    if j == 0:
                        pe.wait_ge(wt_ready, 8 * NT + m + 1)
                        values(8 + h, st1[h % 2], lambda i: sv[:, i, h * 64:(h + 1) * 64], 64, False)
            seen.next(pv_used)
            transpose_tokens()
            project_tokens()
            project_tokens()
            transpose_tokens()
            queries(1)

        @block.scalar
        def _(act):
            seen, step = Seen(act), Chain(act, c_act)
            n_out, n_tr = [0], [0]

            def projected():
                n = n_out[0]
                n_out[0] += 1
                act.wait_ge(pj_done, n + 1)
                return ps[n % 2], pj_free[n % 2]

            def skip(k):
                n_out[0] += k

            def turned(dst):
                n = n_tr[0]
                n_tr[0] += 1
                act.wait_ge(tr_done, n + 1)
                nc.scalar.activation(dst, ps[2 + n % 2].rearrange("p (c n) -> p c n", c=4), ACT.Copy).then_inc(tr_free[n % 2], 1)

            def turn_tokens():
                for t in range(NT):
                    for b in range(2):
                        turned(hT[:, 4 * b:4 * b + 4, t * P:(t + 1) * P])

            def root(n):
                seen.next(var_ready)
                nc.scalar.activation(std[:, 0:n], var[:, 0:n], ACT.Sqrt).then_inc(std_ready, 1)

            def squares(t):
                nc.scalar.activation(hn[:, t, :], x[:, t, :], ACT.Square, accum_out=ss[:, t:t + 1]).then_inc(ss_done, 1)

            def head_out(h, width, at, done):
                act.wait_ge(pv_done, done)
                nc.scalar.activation(hn[:, :, at + h * width:at + (h + 1) * width],
                                     ps[0][:, 0:NT * width].rearrange("p (t n) -> p t n", t=NT), ACT.Copy).then_inc(pv_used, 1)

            for t in range(NT):
                act.wait_ge(x_in, 16 * NT)
                squares(t)
            root(NT)
            act.wait_ge(cst_in, 16 * 13)
            nc.scalar.activation(ccol[:, KC:2 * KC], ccol[:, 0:KC], ACT.Silu).then_inc(act_to_dve, 1)
            seen.next(dve_to_act)
            nc.scalar.activation(lb3[:, 3:5, :], lb3[:, 0:2, :], ACT.Exp).then_inc(act_to_dve, 1)
            turn_tokens()
            for c in range(4):
                bank, free = projected()
                nc.scalar.activation(qT[:, c, :], bank, ACT.Silu).then_inc(free, 1)
            for c in range(4):
                bank, free = projected()
                nc.scalar.activation(kT[:, c, :], bank, ACT.Sigmoid).then_inc(free, 1)
            for t in range(NT):
                bank, free = projected()
                nc.scalar.activation(v1[:, 0, t, :], bank, ACT.Copy).then_inc(free, 1)
            for c in range(4):
                seen.next(dve_to_act)
                nc.scalar.activation(qk[c], cum[:, c, :], ACT.Ln).then_inc(act_to_dve, 1)
            for t in range(NT):
                bank, free = projected()
                nc.scalar.activation(sg1[:, 0, t, :], bank, ACT.Silu).then_inc(free, 1)
            for c in range(4):
                bank, free = projected()
                dst = qT[:, 4 + c, :] if c < 2 else kT[:, 2 + c, :]
                nc.scalar.activation(dst, bank, ACT.Copy, scale=64 ** -0.5 if c < 2 else 1.0).then_inc(free, 1)
            seen.next(low_done)
            nc.scalar.activation(glow, ps[4][0:16, :], ACT.Copy).then_inc(low_copied, 1)
            for t in range(NT):
                bank, free = projected()
                nc.scalar.activation(v1[:, 1, t, :], bank, ACT.Copy).then_inc(free, 1)
            for c in range(2):
                seen.next(dve_to_act)
                step(nc.scalar.activation(qk[4 + c], cum[:, 4 + c, :], ACT.Abs))
                step(nc.scalar.activation(qk[4 + c], qk[4 + c], ACT.Exp, scale=-1.0))
                nc.scalar.activation(qk[4 + c], qk[4 + c], ACT.Ln, bias=1.0).then_inc(act_to_dve, 1)
            for t in range(NT):
                bank, free = projected()
                nc.scalar.activation(sg1[:, 1, t, :], bank, ACT.Silu).then_inc(free, 1)

            n_ex = 0
            h = 0
            for g in range(6):
                for l in range(NQK):
                    seen.next(ex_sub)
                    nc.scalar.activation(ex[n_ex % 3], ex[n_ex % 3], ACT.Exp, scale=1.0 if g < 4 else 1 / 16.0).then_inc(ex_done, 1)
                    n_ex += 1
                for _ in range(1 if g < 4 else 2):
                    act.wait_ge(far_done, h + 1)
                    if h >= 2:
                        act.wait_ge(pv_done, h - 1)
                    st = st1[h % 2]
                    nc.scalar.activation(st[:, 0:2, 256:512], ps[2].rearrange("p (j n) -> p j n", j=2), ACT.Copy)
                    nc.scalar.activation(st[:, 0, P:2 * P], ps[3][:, 0:P], ACT.Copy)
                    nc.scalar.activation(st[:, 2, 3 * P:4 * P], ps[3][:, P:2 * P], ACT.Copy).then_inc(far_copied, 1)
                    if h >= 1:
                        head_out(h - 1, P, 0, h)
                    h += 1
            head_out(7, P, 0, 8)
            act.wait_ge(pv_used, 8)

            def squares_of_heads(n):
                for t in range(NT):
                    if n == 16:
                        seen.next(dve_to_act)
                    nc.scalar.activation(scr, hn[:, t, :], ACT.Square).then_inc(ss_done, 1)
                    root(n)

            def mixed_to_queries(layer):
                turn_tokens()
                skip(2 * NT)
                for t in range(NT):
                    n = n_out[0] - NT + t
                    act.wait_ge(pj_free[n % 2], n // 2 + 1)
                    squares(t)
                root(NT)
                turn_tokens()

            squares_of_heads(8)
            mixed_to_queries(0)

            def queries(layer):
                for m in range(16):
                    bank, free = projected()
                    if m >= 2:
                        act.wait_ge(sc_done, 16 * layer + m - 1)
                    nc.scalar.activation(qst[m % 2], bank, ACT.Copy).then_inc(free, 1)

            def peer_acts(layer):
                seen.next(dve_to_act)
                nc.scalar.activation(gate, gate, ACT.Exp).then_inc(act_to_dve, 1)
                for t in range(NT):
                    base = (layer * NT + t) * GROUPS
                    with act.Fori(0, GROUPS) as i:
                        act.wait_ge(act_in, i + (base + 1))
                        nc.scalar.activation(g8, a8, ACT.Gelu).then_inc(act_out, 1)
                    if layer == 0:
                        seen.next(x_ready)
                        squares(t)
                        root(1)

            queries(0)
            for n in range(12):
                bank, free = projected()
                nc.scalar.activation(modm[:, n * SEC:(n + 1) * SEC], bank, ACT.Copy).then_inc(free, 1)
            peer_acts(0)

            seen.next(dve_to_act)
            nc.scalar.activation(sin, ang, ACT.Sin).then_inc(act_to_dve, 1)
            nc.scalar.activation(cos, ang, ACT.Sin, scale=0.5).then_inc(act_to_dve, 1)
            for t in range(NT):
                squares(t)
            root(NT)
            turn_tokens()
            for dst in (rqT, rkT):
                skip(NT)
                for t in range(NT):
                    turned(dst[:, :, t * P:(t + 1) * P])
            for t in range(NT):
                bank, free = projected()
                nc.scalar.activation(rv[:, t, :], bank, ACT.Copy).then_inc(free, 1)
            for t in range(NT):
                bank, free = projected()
                nc.scalar.activation(rg[:, t, :], bank, ACT.Silu).then_inc(free, 1)
            for dst in (sqT, skT):
                for t in range(NT):
                    bank, free = projected()
                    nc.scalar.activation(sq, bank, ACT.Square).then_inc(ss_done, 1)
                    root(8)
                    if t:
                        turned(dst[:, :, (t - 1) * P:t * P])
                turned(dst[:, :, 3 * P:4 * P])
            for t in range(NT):
                bank, free = projected()
                nc.scalar.activation(sv[:, t, :], bank, ACT.Copy).then_inc(free, 1)
            for h in range(8):
                head_out(h, 64, 0, 8 + h + 1)
            nc.scalar.preload_act_table_set("natural_log_exp_and_others")
            for n in range(8 * NT + 1):
                h, j = n // NT, NT - 1 - n % NT
                if n < 8 * NT:
                    wd = SEQ - j * P
                    z, l = ps[4 + n % 2][:, 0:wd], ab[n % 2][:, 0:wd]
                    act.wait_ge(z_done, 8 * NT + n + 1)
                    if n >= 2:
                        act.wait_ge(z_used, n - 1)
                    step(nc.scalar.activation(l, z, ACT.Abs))
                    step(nc.scalar.activation(l, l, ACT.Exp, scale=-1.0))
                    nc.scalar.activation(l, l, ACT.Ln, bias=1.0).then_inc(ln_ready, 1)
                if n >= 1:
                    m = n - 1
                    h, j = m // NT, NT - 1 - m % NT
                    act.wait_ge(ar_done, m + 1)
                    if j == NT - 1:
                        act.wait_ge(pv_done, 8 + 8 + h - 1)
                    nc.scalar.activation(st1[h % 2][:, j, j * P:SEQ], ps[6 + m % 2][:, 0:SEQ - j * P], ACT.Exp).then_inc(w_exp, 1)
                    if j == 0 and h >= 1:
                        head_out(h - 1, 64, 512, 8 + 8 + h)
            head_out(7, 64, 512, 8 + 8 + 8)
            act.wait_ge(pv_used, 8 + 16)
            squares_of_heads(16)
            mixed_to_queries(1)
            queries(1)
            peer_acts(1)

        @block.vector
        def _(dve):
            seen, step, chosen = Seen(dve), Chain(dve, c_dve), Chain(dve, c_top)
            n_out = [0]
            tt, ts, stt = nc.vector.tensor_tensor, nc.vector.tensor_scalar, nc.vector.scalar_tensor_tensor

            def spread(v, shape):
                while len(v.shape) < len(shape):
                    v = v.unsqueeze(len(v.shape))
                return v.to_broadcast(shape)

            def projected():
                n = n_out[0]
                n_out[0] += 1
                dve.wait_ge(pj_done, n + 1)
                return ps[n % 2], pj_free[n % 2], n // 2 + 1

            def skip(k):
                n_out[0] += k

            def rstd(n, count):
                ts(var[:, 0:n], ss[:, 0:n], 1.0 / count, EPS, ALU.mult, ALU.add).then_inc(var_ready, 1)
                seen.next(var_ready)
                seen.next(std_ready)
                step(nc.vector.reciprocal(rs[:, 0:n], std[:, 0:n]))
                step(tt(nt_[:, 0:n], rs[:, 0:n], rs[:, 0:n], ALU.mult))
                step(tt(nt_[:, 0:n], nt_[:, 0:n], var[:, 0:n], ALU.mult))
                step(ts(nt_[:, 0:n], nt_[:, 0:n], -0.5, 1.5, ALU.mult, ALU.add))
                step(tt(rs[:, 0:n], rs[:, 0:n], nt_[:, 0:n], ALU.mult))

            def normed(gain, shift=None):
                seen.next(ss_done, NT)
                rstd(NT, D)
                for t in range(NT):
                    last = stt(hn[:, t, :], x[:, t, :], rs[:, t:t + 1], gain, ALU.mult, ALU.mult)
                    if shift is not None:
                        step(last)
                        last = tt(hn[:, t, :], hn[:, t, :], shift, ALU.add)
                    last.then_inc(src_ready, 1)

            step(nc.vector.memset(ones, 1.0))
            dve.wait_ge(row_in, 32)
            normed(rows[:, 0, :])
            seen.next(act_to_dve)
            dve.wait_ge(cst_in, 16 * 13)
            step(tt(lb3[:, 2, :], lb3[:, 0, :], lb3[:, 1, :], ALU.max))
            step(tt(lb3[:, 0, :], lb3[:, 0, :], lb3[:, 2, :], ALU.subtract))
            tt(lb3[:, 1, :], lb3[:, 1, :], lb3[:, 2, :], ALU.subtract).then_inc(dve_to_act, 1)
            seen.next(act_to_dve)
            step(tt(lb3[:, 4, :], lb3[:, 4, :], lb3[:, 3, :], ALU.add))
            step(nc.vector.reciprocal(lb3[:, 4, :], lb3[:, 4, :]))
            step(tt(lb3[:, 4, :], lb3[:, 3, :], lb3[:, 4, :], ALU.mult))
            step(ts(lb3[:, 5, :], lb3[:, 4, :], -1.0, 1.0, ALU.mult, ALU.add))

            skip(4)
            for c in range(4):
                n = 4 + c
                dve.wait_ge(pj_free[n % 2], n // 2 + 1)
                step(ts(cum[:, c, :], kT[:, c, :], lb3[:, 5, c:c + 1], lb3[:, 4, c:c + 1], ALU.mult, ALU.add))
                ts(kT[:, c, :], cum[:, c, :], -1.0, 1.0, ALU.mult, ALU.add).then_inc(dve_to_act, 1)
            for c in range(4):
                seen.next(act_to_dve)
                step(nc.vector.tensor_tensor_scan(cum[:, c, :], reset, qk[c], 0.0, ALU.mult, ALU.add))
            for c in range(2):
                dve.wait_ge(low_done, 2)
                ts(cum[:, 4 + c, :], ps[5 + c], bg[:, c:c + 1], None, ALU.add).then_inc(dve_to_act, 1)
            for c in range(2):
                seen.next(act_to_dve)
                step(stt(qk[4 + c], cum[:, 4 + c, :], 0.0, qk[4 + c], ALU.min, ALU.subtract))
                step(nc.vector.tensor_tensor_scan(cum[:, 4 + c, :], reset, qk[4 + c], 0.0, ALU.mult, ALU.add))
            step(nc.vector.tensor_copy(tot.rearrange("p (g c) -> p g c", g=6),
                                       cum.rearrange("p g (c s) -> p g c s", s=CHUNK)[:, :, :, CHUNK - 1]))
            step(nc.vector.memset(rows[:, 2, 512:512 + 144], 0.0))
            T = tot.rearrange("p (g m c) -> p (g m) c", g=6, c=4)
            T8 = tot.rearrange("p (g c) -> p g c", g=6)
            o0 = offs[:, 0].rearrange("p g (m c) -> p (g m) c", c=4)
            o1 = offs[:, 1].rearrange("p g (m c) -> p (g m) c", c=4)
            o2 = offs[:, 2]
            cp = nc.vector.tensor_copy
            step(cp(o0[:, :, 0], T[:, :, 0]))
            step(cp(o0[:, :, 2], T[:, :, 2]))
            step(cp(o1[:, :, 1], T[:, :, 1]))
            step(tt(o1[:, :, 0], T[:, :, 0], T[:, :, 1], ALU.add))
            step(ts(o1[:, :, 3], T[:, :, 2], -1.0, None, ALU.mult))
            step(cp(o2[:, :, 3], T8[:, :, 3]))
            for c in (2, 1, 0):
                step(tt(o2[:, :, c], o2[:, :, c + 1], T8[:, :, c], ALU.add))
            for c in (5, 6, 7):
                step(tt(o2[:, :, c], o2[:, :, c - 1], T8[:, :, c - 1], ALU.subtract))

            FAR = (64, 128, 256)
            spans = (256, 128) + IN_TILE
            assert len(spans) == NQK and spans[2] == 64

            def halves(v, s):
                w = v.rearrange("p (m r s) -> p m r s", r=2, s=s)
                return w[:, :, 0, :], w[:, :, 1, :]

            def exponents(g, l, e):
                s = spans[l]
                if s >= CHUNK:
                    k = s // CHUNK
                    cv = cum[:, g, :].rearrange("p (m r k s) -> p m r k s", r=2, k=k, s=CHUNK)
                    ev = e.rearrange("p (m r k s) -> p m r k s", r=2, k=k, s=CHUNK)
                    ov = offs[:, FAR.index(s), g, :].rearrange("p (m r k) -> p m r k", r=2, k=k)
                    m = SEQ // (2 * s)
                    for r in range(2):
                        o = spread(ov[:, :, r, :], [P, m, k, CHUNK])
                        c = cv[:, :, r, :, :]
                        last = tt(ev[:, :, r, :, :], *((c, o) if r else (o, c)), ALU.subtract)
                    return last
                (ce, co), (ee, eo) = halves(cum[:, g, :], s), halves(e, s)
                edge = spread(ce[:, :, s - 1], [P, SEQ // (2 * s), s])
                tt(ee, edge, ce, ALU.subtract)
                return tt(eo, co, edge, ALU.subtract)

            n_ex = 0

            def decayed(g, l, e):
                seen.next(ex_done)
                (ee, eo), (qe, qo) = halves(e, spans[l]), halves(qk[l], spans[l])
                tt(qe, ee, halves(kT[:, g, :], spans[l])[0], ALU.mult)
                tt(qo, eo, halves(qT[:, g, :], spans[l])[1], ALU.mult).then_inc(qk_ready, 1)

            h = 0
            for g in range(6):
                for l in range(NQK + 1):
                    if l < NQK:
                        if n_ex + l >= 3:
                            dve.wait_ge(qk_ready, n_ex + l - 2)
                        exponents(g, l, ex[(n_ex + l) % 3]).then_inc(ex_sub, 1)
                    if l >= 1:
                        decayed(g, l - 1, ex[(n_ex + l - 1) % 3])
                n_ex += NQK
                for _ in range(1 if g < 4 else 2):
                    for t in range(NT):
                        n = h * NT + t
                        dve.wait_ge(lev_done, n + 1)
                        if t == 0 and h >= 2:
                            dve.wait_ge(pv_done, h - 1)
                        b = 4 + 2 * (n % 2)
                        if n >= 1:
                            dve.wait_ge(st_ready, n)
                        tt(mk, psum[:, b * 512:(b + 2) * 512], levels, ALU.mult).then_inc(lev_used, 1)
                        dve.wait_ge(lev_used, n + 1)
                        nc.vector.tensor_reduce(st1[h % 2][:, t, t * P:(t + 1) * P], mk.rearrange("p (l i) -> p i l", l=NLEV),
                                                AX_X, ALU.add).then_inc(st_ready, 1)
                    h += 1

            def by_head(v, n, width):
                return v.rearrange("p (h n) -> p h n", n=width), [P, n, width]

            dve.wait_ge(pv_used, 8)
            for t in range(NT):
                hv, shape = by_head(hn[:, t, :], 8, P)
                seen.next(ss_done)
                step(nc.vector.tensor_reduce(ss[:, 0:8], by_head(scr, 8, P)[0], AX_X, ALU.add))
                rstd(8, P)
                step(tt(hv, hv, spread(rs[:, 0:8], shape), ALU.mult))
                for m in range(2):
                    half = hn[:, t, m * 512:(m + 1) * 512]
                    g = srow[:, m * P:(m + 1) * P].unsqueeze(1).to_broadcast([P, 4, P])
                    step(tt(by_head(half, 4, P)[0], by_head(half, 4, P)[0], g, ALU.mult))
                    last = tt(half, half, sg1[:, m, t, :], ALU.mult)
                last.then_inc(src_ready, 1)
            skip(24)
            assert n_out[0] == before[7], (n_out, before[7])
            for s in range(2):
                for t in range(NT):
                    bank, free, _ = projected()
                    xs = x[:, t, s * SEC:(s + 1) * SEC]
                    tt(xs, xs, bank, ALU.add).then_inc(free, 1)
            normed(rows[:, 1, :])
            nc.vector.tensor_copy(crep, spread(ccol[:, KC:2 * KC], [P, KC, P])).then_inc(crep_ready, 1)

            def peer(layer):
                if layer == 0:
                    skip(16 + 12)
                else:
                    skip(16)
                for m in range(16):
                    dve.wait_ge(sc_done, 16 * layer + m + 1)
                    nc.vector.tensor_copy(s_all.rearrange("p (t m n) -> p t m n", t=NT, m=16)[:, :, m, :],
                                          ps[4 + m % 2].rearrange("p (t n) -> p t n", t=NT)).then_inc(sc_used, 1)
                dve.wait_ge(sc_used, 16 * (layer + 1))
                with dve.Fori(0, NT) as t:
                    chosen.restart()
                    top_experts(t, chosen)
                nc.vector.tensor_copy(cand[:, 0:1], cand[:, 0:1]).then_inc(dve_to_act, 1)
                seen.next(act_to_dve)
                gv = gate.rearrange("p (h k) -> p h k", k=TOPK)
                step(nc.vector.tensor_reduce(ss[:, 0:NT * NH], gv, AX_X, ALU.add))
                step(nc.vector.reciprocal(rs[:, 0:NT * NH], ss[:, 0:NT * NH]))
                tt(gv, gv, spread(rs[:, 0:NT * NH], [P, NT * NH, TOPK]), ALU.mult).then_inc(top_ready, 1)
                dve.wait_ge(top_ready, layer + 1)
                for t in range(NT):
                    tile_experts(layer, t)

            def top16(step, src, values, places):
                step(nc.vector.max(values[:, 0:8], src))
                step(nc.vector.max_index(places[:, 0:8], values[:, 0:8], src))
                step(nc.vector.match_replace(src, values[:, 0:8], src, NEG))
                step(nc.vector.max(values[:, 8:16], src))
                step(nc.vector.max_index(places[:, 8:16], values[:, 8:16], src))

            def top_experts(t, step):
                step(nc.vector.tensor_copy(stage.rearrange("p m n -> p (m n)"), s_all[:, bass.ds(t * 2048, 2048)]))
                for h in range(NH):
                    for m in range(2):
                        top16(step, stage[:, 2 * h + m, :], tv[:, h, m, :], ti[:, h, m, :])
                    step(tt(cand.rearrange("p (a b) -> p a b", a=TOPK), spread(tv[:, h, 0, :], [P, TOPK, TOPK]),
                            tv[:, h, 1, :].unsqueeze(1).to_broadcast([P, TOPK, TOPK]), ALU.add))
                    top16(step, cand, bv[:, h, :], bp[:, h, :])
                step(nc.vector.tensor_copy(tif, ti))
                bpf = bp.rearrange("p h k -> p (h k)")
                oh3 = onehot.rearrange("p (s k) -> p s k", k=TOPK)
                oh4 = onehot.rearrange("p (h s k) -> p h s k", h=NH, k=TOPK)
                it = iota.unsqueeze(1).to_broadcast([P, SLOTS, TOPK])
                for m, dst in ((0, ia), (1, ib)):
                    if m == 0:
                        step(ts(pai, bpf, 4, None, ALU.logical_shift_right))
                    else:
                        step(ts(pai, bpf, 15, None, ALU.bitwise_and))
                    step(nc.vector.tensor_copy(paf, pai))
                    step(tt(oh3, spread(paf, [P, SLOTS, TOPK]), it, ALU.is_equal))
                    step(tt(oh4, oh4, tif[:, :, m, :].unsqueeze(2).to_broadcast([P, NH, TOPK, TOPK]), ALU.mult))
                    step(nc.vector.tensor_reduce(dst, oh3, AX_X, ALU.add))
                step(stt(idf, ia, float(NKEY), ib, ALU.mult, ALU.add))
                step(nc.vector.tensor_copy(idx[:, bass.ds(t * SLOTS, SLOTS)], idf))
                step(tt(gate[:, bass.ds(t * SLOTS, SLOTS)].rearrange("p (h k) -> p h k", k=TOPK), bv,
                        bv[:, :, 0:1].to_broadcast([P, NH, TOPK]), ALU.subtract))

            def tile_experts(layer, t):
                base = (layer * NT + t) * GROUPS
                step(nc.vector.memset(y, 0.0))
                with dve.Fori(0, GROUPS) as i:
                    for b in range(RING):
                        dve.wait_ge(u_in[b], i * 16 + 16 * (base + 1))
                        nc.vector.tensor_tensor_reduce(out=ur[b], in0=ur[b], in1=hn[:, t, :], scale=1.0, scalar=0.0,
                                                       op0=ALU.mult, op1=ALU.add, accum_out=a8[:, b:b + 1])\
                            .then_inc(u_free, 1)
                    dve.wait_ge(u_free, i * RING + (RING * (base + 2)))
                    dve.sem_inc(act_in, 1)
                    dve.wait_ge(act_out, i + (base + 1))
                    nc.vector.tensor_tensor(c8, g8, gate[:, bass.ds(i * RING + t * SLOTS, RING)], ALU.mult).then_inc(c8_ready, 1)
                    dve.wait_ge(c8_ready, i + (base + 1))
                    for b in range(RING):
                        dve.wait_ge(v_in[b], i * 16 + 16 * (base + 1))
                        stt(y, vr[b], c8[:, b:b + 1], y, ALU.mult, ALU.add).then_inc(v_free, 1)
                        dve.wait_ge(v_free, i * RING + (RING * (base + 1) + b + 1))
                if layer == 0:
                    tt(x[:, t, :], x[:, t, :], y, ALU.add).then_inc(x_ready, 1)
                    dve.wait_ge(x_ready, t + 1)
                    seen.next(ss_done)
                    if t:
                        step(nc.vector.tensor_copy(ss[:, 0:1], ss[:, t:t + 1]))
                    rstd(1, D)
                    step(stt(x[:, t, :], x[:, t, :], rs[:, 0:1], rows[:, 2, :], ALU.mult, ALU.mult))
                else:
                    step(tt(y, y, mod[:, 5, :], ALU.mult))
                    tt(x[:, t, :], x[:, t, :], y, ALU.add).then_inc(out_ready, 1)
                    dve.wait_ge(out_ready, t + 1)

            dve.sem_inc(u_free, RING)
            dve.sem_inc(v_free, RING)
            peer(0)

            step(nc.vector.tensor_copy(posf, pos))
            for t in range(NT):
                step(ts(ang[:, t, :], freq, posf[:, t:t + 1], None, ALU.mult))
            step(ts(turn, ang, 1.0 / TWO_PI, ROUND, ALU.mult, ALU.add))
            step(ts(turn, turn, -ROUND, None, ALU.add))
            for c in two_pi:
                step(stt(ang, turn, -c, ang, ALU.mult, ALU.add))
            ts(ang, ang, 3.1415925, -3.1415925, ALU.min, ALU.max).then_inc(dve_to_act, 1)
            dve.wait_ge(row_in, 16 * 9)
            step(stt(rows[:, 0, :], mod[:, 1, :], 1.0, rows[:, 0, :], ALU.add, ALU.mult))
            step(stt(rows[:, 1, :], mod[:, 4, :], 1.0, rows[:, 1, :], ALU.add, ALU.mult))
            step(ts(srow[:, 512:576], srow[:, 512:576], 64 ** -0.5, None, ALU.mult))
            seen.next(act_to_dve)
            step(ts(nsin, sin, -1.0, None, ALU.mult))
            seen.next(act_to_dve)
            step(tt(cos, cos, cos, ALU.mult))
            step(ts(cos, cos, -2.0, 1.0, ALU.mult, ALU.add))
            normed(rows[:, 0, :], mod[:, 0, :])
            n_rt = 0
            for m in range(2):
                for t in range(NT):
                    bank, free, count = projected()
                    if n_rt >= 2:
                        dve.wait_ge(tr_done, 32 + n_rt - 1)
                    dve.wait_ge(src_ready, 4 * NT + n_rt)
                    r = rt[n_rt % 2]
                    n_rt += 1
                    r4, b4, t4 = [v.rearrange("p (h r n) -> p h r n", h=8, r=2) for v in (r, bank, t3)]
                    tt(r4, b4, cos[:, t, :].unsqueeze(1).unsqueeze(1).to_broadcast([P, 8, 2, 32]), ALU.mult)
                    tt(t4[:, :, 0, :], b4[:, :, 1, :], nsin[:, t, :].unsqueeze(1).to_broadcast([P, 8, 32]), ALU.mult)
                    tt(t4[:, :, 1, :], b4[:, :, 0, :], sin[:, t, :].unsqueeze(1).to_broadcast([P, 8, 32]), ALU.mult)\
                        .then_inc(free, 1)
                    dve.wait_ge(free, count)
                    tt(r, r, t3, ALU.add).then_inc(src_ready, 1)
            skip(2 * NT)
            for m in range(2):
                for t in range(NT):
                    bank, free, count = projected()
                    seen.next(ss_done)
                    step(nc.vector.tensor_reduce(ss[:, 0:8], by_head(sq, 8, 64)[0], AX_X, ALU.add))
                    rstd(8, 64)
                    dve.wait_ge(tr_done, 32 + n_rt - 1)
                    dve.wait_ge(src_ready, 4 * NT + n_rt)
                    r = rt[n_rt % 2]
                    n_rt += 1
                    r3, shape = by_head(r, 8, 64)
                    tt(r3, by_head(bank, 8, 64)[0], spread(rs[:, 0:8], shape), ALU.mult).then_inc(free, 1)
                    dve.wait_ge(free, count)
                    g = srow[:, 512 + 64 * m:576 + 64 * m].unsqueeze(1).to_broadcast(shape)
                    tt(r3, r3, g, ALU.mult).then_inc(src_ready, 1)
            skip(NT)
            for h in range(8):
                dve.wait_ge(dec_in[h % 2], 16 * (h // 2 + 1))
                if h >= 2:
                    dve.wait_ge(pv_done, 8 + h - 1)
                for j in range(NT):
                    n = h * NT + j
                    dve.wait_ge(z_done, n + 1)
                    wd = SEQ - j * P
                    tt(st1[h % 2][:, j, j * P:SEQ], ps[4 + n % 4][:, 0:wd], dec[h % 2][:, 0:wd], ALU.mult).then_inc(wt_ready, 1)
            for n in range(8 * NT + 1):
                if n < 8 * NT:
                    h, j = n // NT, NT - 1 - n % NT
                    wd = SEQ - j * P
                    dve.wait_ge(ln_ready, n + 1)
                    if j == NT - 1:
                        if h >= 2:
                            dve.wait_ge(ar_done, NT * (h - 1))
                        else:
                            dve.wait_ge(z_done, 8 * NT + 1)
                    sv_ = stay[h % 2][:, j, j * P:SEQ]
                    stt(sv_, ps[4 + n % 2][:, 0:wd], 0.0, ab[n % 2][:, 0:wd], ALU.max, ALU.add).then_inc(z_used, 1)
                    dve.wait_ge(z_used, n + 1)
                    sv_ = stay[h % 2][:, j, j * P:(j + 1) * P]
                    tt(sv_, sv_, sticks[:, 2, :], ALU.mult).then_inc(sp_ready, 1)
                if n >= 1:
                    h, j = (n - 1) // NT, NT - 1 - (n - 1) % NT
                    dve.wait_ge(w_exp, n)
                    wv = st1[h % 2][:, j, j * P:(j + 1) * P]
                    tt(wv, wv, sticks[:, 2, :], ALU.mult).then_inc(wt_ready, 1)
            dve.wait_ge(pv_used, 8 + 16)
            for t in range(NT):
                hv, shape = by_head(hn[:, t, :], 16, 64)
                rv_, rshape = by_head(hn[:, t, 0:512], 8, 64)
                step(nc.vector.tensor_reduce(ss[:, 16:24], rv_, AX_X, ALU.add))
                step(ts(ss[:, 16:24], ss[:, 16:24], 1.0 / 64, None, ALU.mult))
                tt(rv_, rv_, spread(ss[:, 16:24], rshape), ALU.subtract).then_inc(dve_to_act, 1)
                seen.next(ss_done)
                step(nc.vector.tensor_reduce(ss[:, 0:16], by_head(scr, 16, 64)[0], AX_X, ALU.add))
                rstd(16, 64)
                step(tt(hv, hv, spread(rs[:, 0:16], shape), ALU.mult))
                step(tt(hn[:, t, 0:512], hn[:, t, 0:512], srow[:, 0:512], ALU.mult))
                tt(hn[:, t, 0:512], hn[:, t, 0:512], rg[:, t, :], ALU.mult)
                sh, sshape = by_head(hn[:, t, 512:1024], 8, 64)
                tt(sh, sh, srow[:, 640:704].unsqueeze(1).to_broadcast(sshape), ALU.mult).then_inc(src_ready, 1)
            for s in range(2):
                for t in range(NT):
                    bank, free, count = projected()
                    cs = slice(s * SEC, (s + 1) * SEC)
                    step(tt(t3, bank, mod[:, 2, cs], ALU.mult))
                    tt(x[:, t, cs], x[:, t, cs], t3, ALU.add).then_inc(free, 1)
                    dve.wait_ge(free, count)
            normed(rows[:, 1, :], mod[:, 3, :])
            peer(1)

        @block.gpsimd
        def _(pool):
            for layer in range(2):
                pool.wait_ge(top_ready, layer + 1)
                for t in range(NT):
                    base = (layer * NT + t) * GROUPS
                    with pool.Fori(0, GROUPS // 2) as i:
                        for j in range(2):
                            slot_free = [pool.to_reg(i * (2 * RING) + ((base + j) * RING + b + 1)) for b in range(RING)]
                            nc.gpsimd.tensor_copy(i8[j], idx[:, bass.ds(i * (2 * RING) + (t * SLOTS + j * RING), RING)])\
                                .then_inc(c_pool, 1)
                            copied = pool.to_reg(i * 2 + (base + j + 1))
                            pool.wait_ge(top_ready, layer + 1)
                            pool.wait_ge(c_pool, copied)
                            for table, ring, free, landed in ((layer_u, ur, u_free, u_in), (layer_v, vr, v_free, v_in)):
                                for b in range(RING):
                                    pool.wait_ge(top_ready, layer + 1)
                                    pool.wait_ge(free, slot_free[b])
                                    nc.gpsimd.indirect_dma_start(ring[b], None, table[layer],
                                                                 bass.IndirectOffsetOnAxis(i8[j][:, b:b + 1], 0))\
                                        .then_inc(landed[b], 16)


_INPUTS = ["x", "norm1_g", "w_in", "hg_lower_logits", "hg_norm_g", "gla_w_gate_up", "gla_b_gate", "gla_norm_g", "w_out",
           "norm2_g", "peer_w_q", "peer_u", "peer_v", "norm_f_g", "c_2", "positions_2", "ada_w_2", "ada_b_2",
           "norm1_gain_2", "norm2_gain_2", "w_in_2", "ret_norm_gain_2", "sb_q_gain_2", "sb_k_gain_2", "sb_out_gain_2",
           "w_out_2", "peer_w_query_2", "peer_down_2", "peer_up_2"]


def kernel(**inputs):
    import concourse.bacc as bacc
    from concourse.bass_utils import run_bass_kernel_spmd

    consts, two_pi = constants()
    data = {}
    for name in _INPUTS:
        v = np.ascontiguousarray(inputs[name])
        if name != "norm_f_g" and name != "hg_lower_logits" and v.shape[0] == 1:
            v = v[0]
        data[name] = v
    for name, key in (("peer_sub_keys", "keysT"), ("peer_sub_keys_2", "keysT_2")):
        data[key] = np.ascontiguousarray(np.asarray(inputs[name])[0].transpose(3, 0, 1, 2).reshape(P, 16 * NKEY))
    data.update(consts)
    nc = bacc.Bacc("TRN2", target_bir_lowering=False, num_devices=1)
    aps = {k: nc.dram_tensor(f"in_{k}", v.shape, mybir.dt.from_np(v.dtype), kind="ExternalInput").ap() for k, v in data.items()}
    out = nc.dram_tensor("out_y", (SEQ, D), F32, kind="ExternalOutput").ap()
    build(nc, aps, out, two_pi)
    r = run_bass_kernel_spmd(nc, [{f"in_{k}": v for k, v in data.items()}], core_ids=[0])
    return r.results[0]["out_y"].reshape(1, SEQ, D)
```

```python
from contextlib import ExitStack

import numpy as np

import concourse.bass as bass
from concourse import mybir

F32 = mybir.dt.float32
U32 = mybir.dt.uint32
I32 = mybir.dt.int32
ALU = mybir.AluOpType
ACT = mybir.ActivationFunctionType
AX_X = mybir.AxisListType.X

P = 128
D = 1024
KC = D // P
SEQ = 512
NT = SEQ // P
SEC = 512
CHUNK = 64
EPS = 1e-6
NH, TOPK, NKEY = 8, 16, 128
SLOTS = NH * TOPK
RING = 4
GATHERED = (0, 1)
DENSE = (2, 3)
ND = len(DENSE) * P
QUARTERS = 4
QA = NKEY // QUARTERS
BODIES = NH
BLOCKS = QA // BODIES
UV = 4
BATCH = 4
BATCHES = ND // BATCH // BODIES
STEP_GROUPS = len(GATHERED) * (NH * TOPK // RING) // (QUARTERS * BODIES)
AHEAD = 8
GROUPS = SLOTS // RING
IN_TILE = (64, 32, 16, 8, 4, 2, 1)
NLEV = len(IN_TILE) + 1
NEG = -3.0e38
TWO_PI = 6.283185307179586
ROUND = 12582912.0


def constants():
    j, i = np.meshgrid(np.arange(P), np.arange(P), indexing="ij")
    levels = [((j // s) % 2 == 0) & (i // s == j // s + 1) for s in IN_TILE] + [i == j]
    rel = np.arange(SEQ)[None, :] - np.arange(P)[:, None]
    gamma = 1.0 - 2.0 ** (-5.0 - np.arange(8))
    decay = np.where(rel >= 0, gamma[:, None, None] ** np.maximum(rel, 0), 0.0) * 64 ** -0.5
    split = 6.28125
    rest = float(np.float32(TWO_PI - split))
    return {
        "c_ident": np.eye(P, dtype=np.float32),
        "c_levels": np.stack(levels, 1).astype(np.float32).reshape(P, NLEV * P),
        "c_reset": np.broadcast_to((np.arange(SEQ) % CHUNK != 0).astype(np.float32), (P, SEQ)).copy(),
        "c_sticks": np.stack([-(j >= i).astype(np.float32), -np.ones((P, P), np.float32),
                              (j < i).astype(np.float32)], 1).reshape(P, 3 * P),
        "c_decay": decay.astype(np.float32),
        "c_freq": np.broadcast_to((10000.0 ** (-np.arange(32) / 32)).astype(np.float32), (P, 32)).copy(),
        "c_keys": np.broadcast_to(np.arange(P, dtype=np.float32), (P, P)).copy(),
        "c_iota": np.broadcast_to(np.arange(16, dtype=np.float32), (P, 16)).copy(),
    }, (split, rest, float(np.float32(TWO_PI - split - rest)))


def by_scalar(batch):
    return batch % 4 != 3


class Chain:

    def __init__(self, eng, sem):
        self.eng, self.sem, self.n = eng, sem, 0

    def restart(self):
        self.eng.sem_clear(self.sem)
        self.n = 0

    def __call__(self, ins, lag=0):
        self.n += 1
        ins.then_inc(self.sem, 1)
        if self.n > lag:
            self.eng.wait_ge(self.sem, self.n - lag)


class Seen:

    def __init__(self, eng):
        self.eng, self.n = eng, {}

    def next(self, sem, by=1):
        self.n[sem.name] = self.n.get(sem.name, 0) + by
        self.eng.wait_ge(sem, self.n[sem.name])


def build(nc, a, out, mod_dram, two_pi):
    with ExitStack() as ctx:
        def sb(name, cols, dt=F32):
            return ctx.enter_context(nc.sbuf_tensor(name, [P, cols], dt))[:, :]

        def sem(name):
            return ctx.enter_context(nc.semaphore(name))

        psum = ctx.enter_context(nc.psum_tensor("psum", [P, 8 * 512], F32))[:, :]
        ps = [psum[:, n * 512:(n + 1) * 512] for n in range(8)]

        x = sb("x", NT * D).rearrange("p (t d) -> p t d", t=NT)
        hn = sb("hn", NT * D).rearrange("p (t d) -> p t d", t=NT)
        hT_ = sb("hT", NT * D)
        hT = hT_.rearrange("p (k n) -> p k n", k=KC)
        w_ = sb("w", 2 * KC * SEC)
        wsec = [w_[:, s * KC * SEC:(s + 1) * KC * SEC].rearrange("p (k n) -> p k n", k=KC) for s in range(2)]
        big = sb("big", 64 * 256)
        modm = sb("mod", 6 * D)
        mod = modm.rearrange("p (r d) -> p r d", r=6)
        rows = sb("rows", 3 * D).rearrange("p (r d) -> p r d", r=3)
        tmp = sb("tmp", 12 * 256)
        srow = sb("srow", 1024)
        lev_ = sb("levels", NLEV * P)
        ident = sb("ident", P)
        small = sb("small", 256)

        def part(base, at_kib, kib, dt=F32):
            v = base[:, int(at_kib * 256):int((at_kib + kib) * 256)]
            return v if dt == F32 else v.bitcast(dt)

        qT = part(big, 0, 12).rearrange("p (g n) -> p g n", g=6)
        kT = part(big, 12, 12).rearrange("p (g n) -> p g n", g=6)
        cum = part(big, 24, 12).rearrange("p (g n) -> p g n", g=6)
        v1 = part(big, 36, 16).rearrange("p (m t n) -> p m t n", m=2, t=NT)
        sg1 = modm[:, 0:4096].rearrange("p (m t n) -> p m t n", m=2, t=NT)
        NQK = len(IN_TILE) + 2
        qk = [part(big, 52 + 2 * n, 2) for n in range(6)] + [modm[:, 4096 + 512 * n:4608 + 512 * n] for n in range(3)]
        st1 = [hT_[:, b * 2048:(b + 1) * 2048].rearrange("p (j n) -> p j n", j=NT) for b in range(2)]
        ex = [part(tmp, 2 * n, 2) for n in range(3)]
        mk = part(tmp, 6, 4)
        reset = part(tmp, 10, 2)
        glow = srow[0:16, 512:1024]
        w_low = rows[:, 2, 0:KC * 16].rearrange("p (k n) -> p k n", k=KC)
        w_up = rows[0:16, 2, 256:512]
        tot = part(small, 0, 0.1875)
        offs = part(rows[:, 2, :], 2, 0.5625).rearrange("p (l g c) -> p l g c", l=3, g=6)
        levels = lev_
        s_all = part(big, 0, 32)
        keysT = part(big, 32, 8).rearrange("p (m n) -> p m n", m=16)
        qst = [part(big, 40 + 2 * b, 2) for b in range(2)]
        onehot = part(modm, 9, 8)
        stage = part(modm, 0, 2).rearrange("p (s n) -> p s n", n=NKEY)
        cand = part(modm, 2, 2).rearrange("p (h n) -> p h n", h=2)
        tv = part(modm, 4, 0.25).rearrange("p (s k) -> p s k", k=TOPK)
        ti = part(modm, 4.25, 0.25, U32)
        hb = part(modm, 4.5, 0.125)
        hp = part(modm, 4.625, 0.125, U32)
        tif = [part(modm, 5 + t, 1) for t in range(NT)]
        ur = [part(w_, 4 * b, 4) for b in range(RING)]
        vr = [part(w_, 16 + 4 * b, 4) for b in range(RING)]
        gates = [part(big, 32 - 32 * b, 32) for b in range(2)]
        ub = [part(modm, 4 * b, 4).rearrange("p (k n) -> p k n", k=KC) for b in range(UV)]
        vb = [rows[:, 0, :], rows[:, 1, :], srow, part(tmp, 0, 4)]
        zero_row = modm[0:1, 4096:4608]
        iaT, nibT, gT = [hT[:, n, 0:ND] for n in range(3)]
        zg = [hT[:, 3 + n, 0:ND] for n in range(4)]
        hits = [part(lev_, 2 * b, 2) for b in range(2)]
        y = ysum = part(tmp, 8, 4)
        bv = [part(tmp, 0.5 * t, 0.5) for t in range(NT)]
        bp = [part(tmp, 2 + 0.5 * t, 0.5, U32) for t in range(NT)]
        pai = part(modm, 17, 0.5, U32)
        paf, ia, ib, idf = [part(modm, 17.5 + 0.5 * n, 0.5) for n in range(4)]
        idx = part(tmp, 4, 2, U32)
        gate = part(tmp, 6, 2)
        rqT, rkT, sqT, skT = [part(big, 8 * n, 8).rearrange("p (g n) -> p g n", g=4) for n in range(4)]
        rv = part(big, 32, 8).rearrange("p (t n) -> p t n", t=NT)
        sv = part(big, 40, 8).rearrange("p (t n) -> p t n", t=NT)
        rg = part(big, 48, 8).rearrange("p (t n) -> p t n", t=NT)
        dec = [part(big, 56 + 2 * b, 2) for b in range(2)]
        sin = part(big, 60, 0.5).rearrange("p (t n) -> p t n", t=NT)
        nsin = part(big, 60.5, 0.5).rearrange("p (t n) -> p t n", t=NT)
        cos = part(big, 61, 0.5).rearrange("p (t n) -> p t n", t=NT)
        ang = part(big, 61.5, 0.5).rearrange("p (t n) -> p t n", t=NT)
        turn = part(big, 62, 0.5).rearrange("p (t n) -> p t n", t=NT)
        rt = [part(tmp, 2 * n, 2) for n in range(2)]
        sq = part(tmp, 4, 2)
        t3 = part(tmp, 6, 2)
        ab = [part(tmp, 2 * n, 2) for n in range(2)]
        stay = [part(big, 8 * n, 8).rearrange("p (j n) -> p j n", j=NT) for n in range(2)]
        scr = [part(tmp, 8 - 4 * b, 4) for b in range(2)]
        pos = small[:, 200:204].bitcast(I32)
        posf = small[:, 204:208]
        freq = small[:, 208:240]
        iota = small[:, 240:256]
        ss = small[:, 0:32]
        var = small[:, 32:64]
        std = small[:, 64:96]
        rs = small[:, 96:128]
        nt_ = small[:, 128:160]
        a8, g8, c8 = [small[:, n:n + RING] for n in (160, 168, 176)]
        i8 = [small[:, 184 + 8 * b:184 + 8 * b + RING].bitcast(U32) for b in range(2)]
        ccol = sb("ccol", 64)
        lb = sb("lb", 64)
        lb3 = lb[:, 0:24].rearrange("p (r h) -> p r h", r=6)
        bg = lb[:, 32:34]
        keyno = sb("key_numbers", P)
        HALF = BATCH * BATCHES // 2
        ga_ = sb("first_keys", 2 * HALF * QA)
        ga = [ga_[:, b * HALF * QA:(b + 1) * HALF * QA].rearrange("p (t a) -> p t a", a=QA) for b in range(2)]
        picks = sb("picks", 2 * BATCH * BATCHES).rearrange("p (r t) -> p r t", r=2)
        y_dense = [psum[:, n * D:(n + 1) * D] for n in range(len(DENSE))]
        sticks = lev_[:, 0:3 * P].rearrange("p (m n) -> p m n", m=3)
        ada_b = [srow[0:1, 512:1024], tmp[0:1, 8 * 256:10 * 256]]
        mod_row = [rows[0:1, 2, 0:SEC], tmp[0:1, 10 * 256:12 * 256]]
        ones = sb("ones", P)

        c_top, c_dve, c_act, c_pool = sem("choice_step"), sem("dve_step"), sem("act_step"), sem("pool_step")
        c_spread, c_picks = sem("spread_step"), sem("picks_step")
        x_in = sem("x_landed")
        cst_in = sem("constants_landed")
        keys_in = sem("keys_landed")
        row_in = sem("rows_landed")
        w_landed = [sem(f"w_landed{s}") for s in range(2)]
        dec_in = [sem(f"decay_landed{s}") for s in range(2)]
        ada_row_in = sem("ada_b_landed")
        pj_done = sem("projected")
        pj_free = [sem(f"projection_read{b}") for b in range(2)]
        tr_done = sem("transposed")
        tr_free = [sem(f"transposed_read{b}") for b in range(2)]
        src_ready = sem("to_transpose")
        ss_done = sem("squares_ready")
        var_ready = sem("variance_ready")
        std_ready = sem("deviation_ready")
        act_to_dve = sem("act_to_dve")
        dve_to_act = sem("dve_to_act")
        x_ready = sem("x_ready")
        ex_sub = sem("exponents_ready")
        ex_done = sem("exponentials_ready")
        qk_ready = sem("decayed_ready")
        lev_done = sem("levels_scored")
        lev_used = sem("levels_masked")
        st_ready = sem("near_scores_ready")
        far_done = sem("far_scored")
        far_copied = sem("far_copied")
        pv_done = sem("values_summed")
        pv_used = sem("values_read")
        low_done = sem("low_rank_done")
        low_copied = sem("low_rank_copied")
        sc_done = sem("keys_scored")
        sc_used = sem("key_scores_copied")
        top_ready = sem("experts_chosen")
        u_in = [sem(f"u_landed{b}") for b in range(RING)]
        v_in = [sem(f"v_landed{b}") for b in range(RING)]
        u_free, v_free = sem("u_slots_free"), sem("v_slots_free")
        act_in, act_out, c8_ready = sem("gelu_wanted"), sem("gelu_ready"), sem("weights_of_group_ready")
        ada_done = sem("modulation_done")
        ada_copied = sem("modulation_copied")
        ada_stored = sem("modulation_stored")
        first_in = sem("first_shift_scale_and_gain_landed")
        mod_in = sem("modulation_landed")
        z_done = sem("sticks_scored")
        z_used = sem("sticks_read")
        ln_ready = sem("softplus_ready")
        sp_ready = sem("stays_ready")
        ar_done = sem("stick_logs_summed")
        w_exp = sem("weights_raised")
        wt_ready = sem("weights_ready")
        picks_ready = sem("dense_picks_ready")
        picks_turned = sem("dense_picks_turned")
        picks_copied = sem("dense_picks_copied")
        all_chosen = sem("all_experts_chosen")
        ub_in = [sem(f"u_block_landed{b}") for b in range(UV)]
        vb_in = [sem(f"v_block_landed{b}") for b in range(UV)]
        blk_done, blk_gelu = sem("block_multiplied"), sem("block_gelu_ready")
        blk_ready, blk_summed = sem("block_weighed"), sem("block_summed")
        hit_ready, ga_ready = sem("second_keys_spread"), sem("first_keys_spread")
        hit_by_vector = sem("second_keys_spread_by_vector")
        ga_used, ga_copied = sem("gates_multiplied"), sem("gates_copied")
        dense_done = sem("dense_done")
        out_ready = sem("out_ready")
        out_done = sem("out_stored")

        def cols(w, k):
            return [(w, s * SEC) for s in range(k)]

        w_in1 = a["w_in"]
        order = [(w_in1, 0), (w_in1, 512), (w_in1, 1024), (w_in1, 1536), (w_in1, 2048), (w_in1, 2560), (w_in1, 3088)]
        ada = cols(a["ada_w_2"], 12)
        ada_at = [len(order) + n + (6 if n >= NH else 0) for n in range(12)]
        order += ada[:NH] + cols(a["w_out"], 2) + cols(a["peer_w_q"], 4) + ada[NH:]
        order += cols(a["w_in_2"], 7) + cols(a["w_out_2"], 2) + cols(a["peer_w_query_2"], 4)
        outputs = [0 if n in ada_at else 4 for n in range(len(order))]
        before = [sum(outputs[:n]) for n in range(len(order) + 1)]

        layer_u = [a["peer_u"], a["peer_down_2"]]
        layer_v = [a["peer_v"], a["peer_up_2"]]
        layer_uT = [a["uT"], a["uT_2"]]
        layer_keys = [a["keysT"], a["keysT_2"]]
        block = ctx.enter_context(nc.Block())

        @block.sync
        def _(sp):
            def load_section(n):
                w, at = order[n]
                if n >= 2:
                    if n - 2 in ada_at:
                        sp.wait_ge(ada_done, ada_at.index(n - 2) + 1)
                    else:
                        sp.wait_ge(pj_done, before[n - 1])
                sp.dma_start(wsec[n % 2], w[:, at:at + SEC].rearrange("(k p) n -> p k n", p=P)).then_inc(w_landed[n % 2], 16)

            def expert_blocks(layer):
                sp.wait_ge(all_chosen, layer + 1)
                with sp.Fori(0, NKEY // UV) as i:
                    for b in range(UV):
                        at = layer * NKEY + AHEAD + 1 - UV + b
                        sp.wait_ge(blk_done, i * UV + at)
                        sp.dma_start(ub[b], layer_uT[layer][:, bass.ds(i * (UV * D) + b * D, D)]
                                     .rearrange("p (k n) -> p k n", k=KC)).then_inc(ub_in[b], 16)
                        sp.wait_ge(blk_summed, i * UV + at)
                        sp.dma_start(vb[b], layer_v[layer][bass.ds(i * (UV * P) + b * P, P), :]).then_inc(vb_in[b], 16)

            for t in range(NT):
                sp.dma_start(x[:, t, :], a["x"][t * P:(t + 1) * P, :]).then_inc(x_in, 16)
            sp.dma_start(rows[:, 0, :], a["norm1_g"].partition_broadcast(P)).then_inc(row_in, 16)
            sp.dma_start(ident, a["c_ident"]).then_inc(cst_in, 16)
            sp.dma_start(levels, a["c_levels"]).then_inc(cst_in, 16)
            sp.dma_start(reset, a["c_reset"]).then_inc(cst_in, 16)
            sp.dma_start(iota, a["c_iota"]).then_inc(cst_in, 16)
            sp.dma_start(keyno, a["c_keys"]).then_inc(cst_in, 16)
            sp.dma_start(freq, a["c_freq"]).then_inc(cst_in, 16)
            sp.dma_start(w_low, a["w_in"][:, 3072:3088].rearrange("(k p) n -> p k n", p=P)).then_inc(cst_in, 16)
            sp.dma_start(w_up, a["gla_w_gate_up"]).then_inc(cst_in, 16)
            with nc.allow_non_contiguous_dma(reason="a few hundred values, one to a partition"):
                sp.dma_start(lb3[:, 0:2, :], a["hg_lower_logits"].rearrange("r (h p) -> p r h", p=P)).then_inc(cst_in, 16)
                sp.dma_start(bg, a["gla_b_gate"].rearrange("(h p) -> p h", p=P)).then_inc(cst_in, 16)
                sp.dma_start(ccol[:, 0:KC], a["c_2"].rearrange("(k p) -> p k", p=P)).then_inc(cst_in, 16)
                sp.dma_start(pos, a["positions_2"].rearrange("(t p) -> p t", p=P)).then_inc(cst_in, 16)
            sp.dma_start(srow[:, 0:128], a["hg_norm_g"].partition_broadcast(P)).then_inc(cst_in, 16)
            sp.dma_start(srow[:, 128:256], a["gla_norm_g"].partition_broadcast(P)).then_inc(cst_in, 16)
            sp.dma_start(rows[:, 1, :], a["norm2_g"].partition_broadcast(P)).then_inc(row_in, 16)
            def modulation(n):
                if n:
                    sp.wait_ge(ada_done, n)
                sp.dma_start(ada_b[n // NH], a["ada_b_2"][None, n * SEC:(n + 1) * SEC]).then_inc(ada_row_in, 16)
                if ada_at[n] + 2 < 25:
                    load_section(ada_at[n] + 2)
                sp.wait_ge(ada_copied, n + 1)
                sp.dma_start(mod_dram[:, n * SEC:(n + 1) * SEC], mod_row[n // NH]).then_inc(ada_stored, 16)

            for n in range(9):
                load_section(n)
            sp.wait_ge(low_done, 2)
            for n in range(NH):
                modulation(n)
            sp.wait_ge(pv_used, 8)
            sp.wait_ge(ada_stored, 16 * NH)
            sp.dma_start(keysT, layer_keys[0].rearrange("d (m n) -> d m n", m=16)).then_inc(keys_in, 16)
            sp.dma_start(rows[:, 2, :], a["norm_f_g"].partition_broadcast(P)).then_inc(keys_in, 16)
            for n in range(17, 23):
                load_section(n)
            sp.wait_ge(src_ready, 2 * NT)
            for n in range(NH, 12):
                modulation(n)
            sp.wait_ge(ada_stored, 16 * 12)
            expert_blocks(0)
            sp.wait_ge(dense_done, 1)
            sp.dma_start(modm[:, 0:2 * D], mod_dram[0, 0:2 * D].partition_broadcast(P)).then_inc(first_in, 16)
            sp.dma_start(rows[:, 0, :], a["norm1_gain_2"].partition_broadcast(P)).then_inc(first_in, 16)
            sp.wait_ge(v_free, RING + len(GATHERED) * SLOTS)
            load_section(25)
            load_section(26)
            sp.dma_start(modm[:, 2 * D:], mod_dram[0, 2 * D:].partition_broadcast(P)).then_inc(mod_in, 16)
            sp.dma_start(rows[:, 1, :], a["norm2_gain_2"].partition_broadcast(P)).then_inc(row_in, 16)
            sp.dma_start(srow[:, 0:512], a["ret_norm_gain_2"].partition_broadcast(P)).then_inc(row_in, 16)
            sp.dma_start(srow[:, 512:576], a["sb_q_gain_2"].partition_broadcast(P)).then_inc(row_in, 16)
            sp.dma_start(srow[:, 576:640], a["sb_k_gain_2"].partition_broadcast(P)).then_inc(row_in, 16)
            sp.dma_start(srow[:, 640:704], a["sb_out_gain_2"].partition_broadcast(P)).then_inc(row_in, 16)
            sp.dma_start(lev_[:, 0:3 * P], a["c_sticks"]).then_inc(row_in, 16)
            for n in range(27, 32):
                load_section(n)
            for h in range(8):
                if h >= 2:
                    sp.wait_ge(wt_ready, NT * (h - 1))
                else:
                    sp.wait_ge(blk_ready, NKEY)
                sp.dma_start(dec[h % 2], a["c_decay"][h]).then_inc(dec_in[h % 2], 16)
            load_section(32)
            load_section(33)
            sp.wait_ge(pv_used, 8 + 16)
            sp.dma_start(keysT, layer_keys[1].rearrange("d (m n) -> d m n", m=16)).then_inc(keys_in, 16)
            for n in range(34, 38):
                load_section(n)
            expert_blocks(1)
            for t in range(NT):
                sp.wait_ge(out_ready, t + 1)
                sp.dma_start(out[t * P:(t + 1) * P, :], x[:, t, :]).then_inc(out_done, 16)
            sp.wait_ge(out_done, 16 * NT)

        @block.tensor
        def _(pe):
            seen = Seen(pe)
            n_out, n_tr, n_sec = [0], [0], [0]

            def next_bank():
                n = n_out[0]
                n_out[0] += 1
                if n >= 2:
                    pe.wait_ge(pj_free[n % 2], n // 2)
                return ps[n % 2]

            def section():
                n = n_sec[0]
                n_sec[0] += 1
                pe.wait_ge(w_landed[n % 2], 16 * (n // 2 + 1))
                return wsec[n % 2]

            def project_tokens():
                w = section()
                for t in range(NT):
                    bank = next_bank()
                    for k in range(KC):
                        last = nc.tensor.matmul(bank, hT[:, k, t * P:(t + 1) * P], w[:, k, :], start=k == 0, stop=k == KC - 1)
                    last.then_inc(pj_done, 1)

            def project_columns():
                w = section()
                for c in range(SEC // P):
                    bank = next_bank()
                    for k in range(KC):
                        last = nc.tensor.matmul(bank, w[:, k, c * P:(c + 1) * P], hT[:, k, :], start=k == 0, stop=k == KC - 1)
                    last.then_inc(pj_done, 1)

            def transpose4(blocks):
                n = n_tr[0]
                n_tr[0] += 1
                if n >= 2:
                    pe.wait_ge(tr_free[n % 2], n // 2)
                for b, s in enumerate(blocks):
                    last = nc.tensor.transpose(ps[2 + n % 2][:, b * P:(b + 1) * P], s, ident)
                last.then_inc(tr_done, 1)

            def transposes_read():
                for b in range(2):
                    pe.wait_ge(tr_free[b], n_tr[0] // 2)

            def transpose_tokens():
                for t in range(NT):
                    seen.next(src_ready)
                    for b in range(2):
                        transpose4([hn[:, t, (4 * b + c) * P:(4 * b + c + 1) * P] for c in range(4)])
                transposes_read()

            def queries(layer):
                pe.wait_ge(keys_in, 16 * (2 + layer))

                def scores_of(m):
                    n = n_out[0] - 1 if m < 15 else n_out[0]
                    n -= 1
                    pe.wait_ge(pj_free[n % 2], n // 2 + 1)
                    if m >= 4:
                        pe.wait_ge(sc_used, 16 * layer + m - 3)
                    for t in range(NT):
                        last = nc.tensor.matmul(ps[4 + m % 4][:, t * P:(t + 1) * P], qst[m % 2][:, t * P:(t + 1) * P],
                                                keysT[:, m, :], start=True, stop=True)
                    last.then_inc(sc_done, 1)

                for s in range(4):
                    w = section()
                    for c in range(4):
                        bank = next_bank()
                        for k in range(KC):
                            last = nc.tensor.matmul(bank, w[:, k, c * P:(c + 1) * P], hT[:, k, :],
                                                    start=k == 0, stop=k == KC - 1)
                        last.then_inc(pj_done, 1)
                        if 4 * s + c:
                            scores_of(4 * s + c - 1)
                scores_of(15)

            def dense_experts(layer):
                for n in range(len(DENSE)):
                    pe.wait_ge(picks_ready, len(DENSE) * layer + n + 1)
                    for r, v in enumerate((ia, ib, gate[:, DENSE[n] * SLOTS:(DENSE[n] + 1) * SLOTS])):
                        last = nc.tensor.transpose(ps[6 + n][:, r * P:(r + 1) * P], v, ident)
                    last.then_inc(picks_turned, 1)
                pe.wait_ge(picks_copied, layer + 1)
                turned = layer + 1

                def held(s, value):
                    pe.wait_ge(picks_copied, turned)
                    pe.wait_ge(s, value)

                def spread_batch(q, i, n):
                    at = (layer * QUARTERS + q) * BODIES * BATCHES + n
                    mine = sum(by_scalar(b) for b in range(BATCHES))
                    earlier = layer * ((QUARTERS - 1) * BATCHES + mine) * BODIES
                    if q:
                        held(hit_ready, i * BATCHES + (earlier + ((q - 1) * BATCHES + mine) * BODIES + n + 1))
                    elif by_scalar(n):
                        held(hit_ready, i * mine + (earlier + sum(by_scalar(b) for b in range(n + 1))))
                    else:
                        held(hit_by_vector, i * (BATCHES - mine) + (layer * (BATCHES - mine) * BODIES
                                                                    + sum(not by_scalar(b) for b in range(n + 1))))
                    if n % 4 == 0:
                        held(ga_ready, i * 2 + (at // 4 + 1))
                        held(ga_copied, i * 2 + ((layer * QUARTERS + q) * BODIES * 2 + n // 4 + AHEAD - 1))
                    for j in range(BATCH):
                        c = (n % 4 * BATCH + j) * QA
                        last = nc.tensor.matmul(ps[6 + n // 4][:, c:c + QA], hits[n % 2][:, j * P:(j + 1) * P],
                                                ga[n // 4][:, n % 4 * BATCH + j, :], start=True, stop=True)
                    last.then_inc(ga_used, 1)

                def block_in(e, i):
                    at = layer * NKEY + e
                    held(ub_in[e % UV], i * (BLOCKS // UV * 16) + (16 * (at // UV) + 16))
                    held(blk_gelu, i * BLOCKS + (at + AHEAD - 1))
                    for k in range(KC):
                        last = nc.tensor.matmul(ps[4 + e % 2][:, 0:ND], ub[e % UV][:, k, :], hT[:, k, ND:SEQ],
                                                start=k == 0, stop=k == KC - 1)
                    last.then_inc(blk_done, 1)

                def block_out(e, i):
                    at = layer * NKEY + e
                    held(vb_in[e % UV], i * (BLOCKS // UV * 16) + (16 * (at // UV) + 16))
                    held(blk_ready, i * BLOCKS + (at + 1))
                    for n in range(len(DENSE)):
                        for c in range(2):
                            last = nc.tensor.matmul(y_dense[n][:, c * 512:(c + 1) * 512], zg[e % 4][:, n * P:(n + 1) * P],
                                                    vb[e % UV][:, c * 512:(c + 1) * 512], start=False, stop=False)
                    last.then_inc(blk_summed, 1)

                with pe.Fori(0, BODIES) as i:
                    for n in range(BATCHES):
                        spread_batch(0, i, n)
                pe.wait_ge(all_chosen, layer + 1)
                for b in range(4):
                    nc.tensor.matmul(ps[b], ones[0:1, :], zero_row, start=True, stop=False)
                block_in(0, 0)
                block_in(1, 0)

                def step_(q, i, last_step=False):
                    for j in range(BLOCKS):
                        e = q * QA + j
                        if not (last_step and j >= BLOCKS - 2):
                            block_in(e + 2, i)
                        block_out(e, i)
                        if q + 1 < QUARTERS:
                            spread_batch(q + 1, i, 2 * j)
                            spread_batch(q + 1, i, 2 * j + 1)

                for q in range(QUARTERS):
                    last = q == QUARTERS - 1
                    with pe.Fori(0, BODIES - last) as i:
                        step_(q, i)
                    if last:
                        step_(q, BODIES - 1, True)
                for b in range(4):
                    done = nc.tensor.matmul(ps[b], ones[0:1, :], zero_row, start=False, stop=True)
                done.then_inc(dense_done, 1)
                if layer == 0:
                    pe.wait_ge(x_ready, NT)

            pe.sem_inc(blk_done, AHEAD)
            pe.sem_inc(blk_summed, AHEAD)
            pe.sem_inc(ga_used, AHEAD)

            seen.next(cst_in, 16 * 14)
            transpose_tokens()
            project_columns()
            project_columns()
            project_tokens()
            project_tokens()
            project_columns()
            for k in range(KC):
                last = nc.tensor.matmul(ps[4][0:16, :], w_low[:, k, :], hT[:, k, :], start=k == 0, stop=k == KC - 1)
            last.then_inc(low_done, 1)
            project_tokens()
            seen.next(low_copied)
            for c in range(2):
                last = nc.tensor.matmul(ps[5 + c], w_up[:, c * P:(c + 1) * P], glow, start=True, stop=True)
            last.then_inc(low_done, 1)
            project_tokens()

            def mix1(g, h, prt):
                if h >= 1:
                    pe.wait_ge(far_copied, h)
                q256, q128 = qk[0][prt], qk[1][prt]
                nc.tensor.matmul(ps[2][:, 0:256], q256[:, 0:P], q256[:, 256:512], start=True, stop=True)
                nc.tensor.matmul(ps[2][:, 256:512], q256[:, P:2 * P], q256[:, 256:512], start=True, stop=True)
                nc.tensor.matmul(ps[3][:, 0:P], q128[:, 0:P], q128[:, P:2 * P], start=True, stop=True)
                nc.tensor.matmul(ps[3][:, P:2 * P], q128[:, 2 * P:3 * P], q128[:, 3 * P:4 * P], start=True, stop=True)\
                    .then_inc(far_done, 1)
                for t in range(NT):
                    n = h * NT + t
                    if n >= 2:
                        pe.wait_ge(lev_used, n - 1)
                    tt = slice(t * P, (t + 1) * P)
                    for l in range(NLEV):
                        lhs, rhs = (qk[2 + l], qk[2 + l]) if l < NLEV - 1 else (kT[:, g, :], qT[:, g, :])
                        last = nc.tensor.matmul(ps[4 + 2 * (n % 2) + l // 4][:, (l % 4) * P:(l % 4 + 1) * P],
                                                lhs[prt][:, tt], rhs[prt][:, tt], start=True, stop=True)
                    last.then_inc(lev_done, 1)

            def values(h, st, v_of, width, first=False):
                if not first:
                    seen.next(pv_used)
                for t in range(NT):
                    for j in range(t + 1):
                        last = nc.tensor.matmul(ps[0][:, t * width:(t + 1) * width], st[:, j, t * P:(t + 1) * P], v_of(j),
                                                start=j == 0, stop=j == t)
                last.then_inc(pv_done, 1)

            def values1(h):
                pe.wait_ge(st_ready, (h + 1) * NT)
                pe.wait_ge(far_copied, h + 1)
                m, c = (0, h) if h < 4 else (1, h - 4)
                values(h, st1[h % 2], lambda j: v1[:, m, j, c * P:(c + 1) * P], P, first=h == 0)

            def modulation(n):
                if n in (0, NH):
                    pe.wait_ge(pj_free[1], n_out[0] // 2)
                w = section()
                if n >= 1:
                    pe.wait_ge(ada_copied, n)
                for k in range(KC):
                    nc.tensor.matmul(ps[1][0:1, :], ccol[:, KC + k:KC + k + 1], w[:, k, :], start=k == 0, stop=False)
                seen.next(ada_row_in, 16)
                nc.tensor.matmul(ps[1][0:1, :], ones[0:1, 0:1], ada_b[n // NH], start=False, stop=True).then_inc(ada_done, 1)

            full, heads = slice(0, P), [slice(0, 64), slice(64, P)]
            of_group = [(g, full) for g in range(4)] + [(4 + n // 2, heads[n % 2]) for n in range(4)]
            pe.wait_ge(pj_free[0], (n_out[0] + 1) // 2)
            for h, (g, prt) in enumerate(of_group):
                if h < 4 or h % 2 == 0:
                    seen.next(qk_ready, NQK)
                mix1(g, h, prt)
                if h >= 1:
                    values1(h - 1)
                modulation(h)
            values1(7)
            seen.next(pv_used)
            transpose_tokens()
            project_tokens()
            project_tokens()
            transpose_tokens()
            queries(0)
            for n in range(NH, 12):
                modulation(n)
            dense_experts(0)

            transpose_tokens()

            def project_and_turn():
                w = section()
                for t in range(NT):
                    bank = next_bank()
                    for k in range(KC):
                        last = nc.tensor.matmul(bank, hT[:, k, t * P:(t + 1) * P], w[:, k, :], start=k == 0, stop=k == KC - 1)
                    last.then_inc(pj_done, 1)
                    if t:
                        turn_one()
                turn_one()

            n_turn = [0]

            def turn_one():
                r = rt[n_turn[0] % 2]
                n_turn[0] += 1
                seen.next(src_ready)
                transpose4([r[:, c * P:(c + 1) * P] for c in range(4)])

            project_and_turn()
            project_and_turn()
            project_tokens()
            project_tokens()
            project_and_turn()
            project_and_turn()
            project_tokens()
            transposes_read()
            pe.wait_ge(pj_free[0], (n_out[0] + 1) // 2)
            pe.wait_ge(pj_free[1], n_out[0] // 2)
            for h in range(8):
                prt = heads[h % 2]
                for j in range(NT):
                    n = h * NT + j
                    if n >= 4:
                        pe.wait_ge(wt_ready, n - 3)
                    nc.tensor.matmul(ps[4 + n % 4][:, 0:SEQ - j * P], rkT[prt, h // 2, j * P:(j + 1) * P],
                                     rqT[prt, h // 2, j * P:SEQ], start=True, stop=True).then_inc(z_done, 1)
                if h >= 1:
                    pe.wait_ge(wt_ready, h * NT)
                    values(h - 1, st1[(h - 1) % 2], lambda j: rv[:, j, (h - 1) * 64:h * 64], 64, first=h == 1)
            pe.wait_ge(wt_ready, 8 * NT)
            values(7, st1[1], lambda j: rv[:, j, 448:512], 64)

            def score(h, j, bank, start, stop):
                prt = heads[h % 2]
                return nc.tensor.matmul(bank[:, 0:SEQ - j * P], skT[prt, h // 2, j * P:(j + 1) * P],
                                        sqT[prt, h // 2, j * P:SEQ], start=start, stop=stop)

            for n in range(8 * NT + 1):
                h, j = n // NT, NT - 1 - n % NT
                if n < 8 * NT:
                    if n >= 2:
                        pe.wait_ge(z_used, n - 1)
                    score(h, j, ps[4 + n % 2], True, True).then_inc(z_done, 1)
                if n >= 1:
                    m = n - 1
                    h, j = m // NT, NT - 1 - m % NT
                    pe.wait_ge(sp_ready, m + 1)
                    if m >= 2:
                        pe.wait_ge(wt_ready, 8 * NT + m - 1)
                    bank = ps[6 + m % 2]
                    score(h, j, bank, True, False)
                    for i in range(NT - 1, j - 1, -1):
                        last = nc.tensor.matmul(bank[:, (i - j) * P:SEQ - j * P], sticks[:, 0 if i == j else 1, :],
                                                stay[h % 2][:, i, i * P:SEQ], start=False, stop=i == j)
                    last.then_inc(ar_done, 1)
                    if j == 0:
                        pe.wait_ge(wt_ready, 8 * NT + m + 1)
                        values(8 + h, st1[h % 2], lambda i: sv[:, i, h * 64:(h + 1) * 64], 64, False)
            seen.next(pv_used)
            transpose_tokens()
            project_tokens()
            project_tokens()
            transpose_tokens()
            queries(1)
            dense_experts(1)

        @block.scalar
        def _(act):
            seen, step, steps = Seen(act), Chain(act, c_act), Chain(act, c_spread)
            n_out, n_tr = [0], [0]

            def projected():
                n = n_out[0]
                n_out[0] += 1
                act.wait_ge(pj_done, n + 1)
                return ps[n % 2], pj_free[n % 2]

            def skip(k):
                n_out[0] += k

            def turned(dst):
                n = n_tr[0]
                n_tr[0] += 1
                act.wait_ge(tr_done, n + 1)
                nc.scalar.activation(dst, ps[2 + n % 2].rearrange("p (c n) -> p c n", c=4), ACT.Copy).then_inc(tr_free[n % 2], 1)

            def turn_tokens():
                for t in range(NT):
                    for b in range(2):
                        turned(hT[:, 4 * b:4 * b + 4, t * P:(t + 1) * P])

            def root(n):
                seen.next(var_ready)
                nc.scalar.activation(std[:, 0:n], var[:, 0:n], ACT.Sqrt).then_inc(std_ready, 1)

            def squares(t):
                nc.scalar.activation(hn[:, t, :], x[:, t, :], ACT.Square, accum_out=ss[:, t:t + 1]).then_inc(ss_done, 1)

            def head_out(h, width, at, done):
                act.wait_ge(pv_done, done)
                nc.scalar.activation(hn[:, :, at + h * width:at + (h + 1) * width],
                                     ps[0][:, 0:NT * width].rearrange("p (t n) -> p t n", t=NT), ACT.Copy).then_inc(pv_used, 1)

            for t in range(NT):
                act.wait_ge(x_in, 16 * NT)
                squares(t)
            root(NT)
            act.wait_ge(cst_in, 16 * 14)
            nc.scalar.activation(ccol[:, KC:2 * KC], ccol[:, 0:KC], ACT.Silu).then_inc(act_to_dve, 1)
            seen.next(dve_to_act)
            nc.scalar.activation(lb3[:, 3:5, :], lb3[:, 0:2, :], ACT.Exp).then_inc(act_to_dve, 1)
            turn_tokens()
            for c in range(4):
                bank, free = projected()
                nc.scalar.activation(qT[:, c, :], bank, ACT.Silu).then_inc(free, 1)
            for c in range(4):
                bank, free = projected()
                nc.scalar.activation(kT[:, c, :], bank, ACT.Sigmoid).then_inc(free, 1)
            for t in range(NT):
                bank, free = projected()
                nc.scalar.activation(v1[:, 0, t, :], bank, ACT.Copy).then_inc(free, 1)
            for c in range(4):
                seen.next(dve_to_act)
                nc.scalar.activation(qk[c], cum[:, c, :], ACT.Ln).then_inc(act_to_dve, 1)
            for t in range(NT):
                bank, free = projected()
                nc.scalar.activation(sg1[:, 0, t, :], bank, ACT.Silu).then_inc(free, 1)
            for c in range(4):
                bank, free = projected()
                dst = qT[:, 4 + c, :] if c < 2 else kT[:, 2 + c, :]
                nc.scalar.activation(dst, bank, ACT.Copy, scale=64 ** -0.5 if c < 2 else 1.0).then_inc(free, 1)
            seen.next(low_done)
            nc.scalar.activation(glow, ps[4][0:16, :], ACT.Copy).then_inc(low_copied, 1)
            for t in range(NT):
                bank, free = projected()
                nc.scalar.activation(v1[:, 1, t, :], bank, ACT.Copy).then_inc(free, 1)
            for c in range(2):
                seen.next(dve_to_act)
                step(nc.scalar.activation(qk[4 + c], cum[:, 4 + c, :], ACT.Abs))
                step(nc.scalar.activation(qk[4 + c], qk[4 + c], ACT.Exp, scale=-1.0))
                nc.scalar.activation(qk[4 + c], qk[4 + c], ACT.Ln, bias=1.0).then_inc(act_to_dve, 1)
            for t in range(NT):
                bank, free = projected()
                nc.scalar.activation(sg1[:, 1, t, :], bank, ACT.Silu).then_inc(free, 1)

            def modulation(n):
                act.wait_ge(ada_done, n + 1)
                if n:
                    act.wait_ge(ada_stored, 16 * n)
                nc.scalar.activation(mod_row[n // NH], ps[1][0:1, :], ACT.Copy).then_inc(ada_copied, 1)

            n_ex = 0
            h = 0
            for g in range(6):
                for l in range(NQK):
                    if l == 6 and h:
                        modulation(h - 1)
                    seen.next(ex_sub)
                    nc.scalar.activation(ex[n_ex % 3], ex[n_ex % 3], ACT.Exp, scale=1.0 if g < 4 else 1 / 16.0).then_inc(ex_done, 1)
                    n_ex += 1
                for second in range(1 if g < 4 else 2):
                    if second:
                        modulation(h - 1)
                    act.wait_ge(far_done, h + 1)
                    if h >= 2:
                        act.wait_ge(pv_done, h - 1)
                    st = st1[h % 2]
                    nc.scalar.activation(st[:, 0:2, 256:512], ps[2].rearrange("p (j n) -> p j n", j=2), ACT.Copy)
                    nc.scalar.activation(st[:, 0, P:2 * P], ps[3][:, 0:P], ACT.Copy)
                    nc.scalar.activation(st[:, 2, 3 * P:4 * P], ps[3][:, P:2 * P], ACT.Copy).then_inc(far_copied, 1)
                    if h >= 1:
                        head_out(h - 1, P, 0, h)
                    h += 1
            modulation(7)
            head_out(7, P, 0, 8)
            act.wait_ge(pv_used, 8)

            def squares_of_heads(n):
                for t in range(NT + 1):
                    if t < NT:
                        if n == 16:
                            seen.next(dve_to_act)
                        nc.scalar.activation(scr[t % 2], hn[:, t, :], ACT.Square).then_inc(ss_done, 1)
                    if t:
                        root(n)

            def mixed_to_queries(layer):
                turn_tokens()
                skip(2 * NT)
                for t in range(NT):
                    n = n_out[0] - NT + t
                    act.wait_ge(pj_free[n % 2], n // 2 + 1)
                    squares(t)
                root(NT)
                turn_tokens()

            squares_of_heads(8)
            mixed_to_queries(0)

            def queries(layer):
                for m in range(16):
                    bank, free = projected()
                    if m >= 2:
                        act.wait_ge(sc_done, 16 * layer + m - 1)
                    nc.scalar.activation(qst[m % 2], bank, ACT.Copy).then_inc(free, 1)

            def gate_exp(t):
                seen.next(dve_to_act)
                nc.scalar.activation(gate[:, t * SLOTS:(t + 1) * SLOTS], gate[:, t * SLOTS:(t + 1) * SLOTS], ACT.Exp)\
                    .then_inc(act_to_dve, 1)

            def peer_acts(layer):
                for n, t in enumerate(DENSE):
                    gate_exp(t)
                    act.wait_ge(picks_turned, len(DENSE) * layer + n + 1)
                    cols = slice(n * P, (n + 1) * P)
                    nc.scalar.activation(iaT[:, cols], ps[6 + n][:, 0:P], ACT.Copy)
                    nc.scalar.activation(nibT[:, cols], ps[6 + n][:, P:2 * P], ACT.Copy, scale=-1.0)
                    last = nc.scalar.activation(gT[:, cols], ps[6 + n][:, 2 * P:3 * P], ACT.Copy)
                last.then_inc(picks_copied, 1)
                act.wait_ge(picks_copied, layer + 1)

                def held(s, value):
                    act.wait_ge(picks_copied, layer + 1)
                    act.wait_ge(s, value)

                def step_picks(i):
                    steps.restart()
                    steps(nc.scalar.activation(picks[:, 0, :], nibT[:, bass.ds(i * (BATCH * BATCHES), BATCH * BATCHES)], ACT.Copy))

                def spread_batch(q, i, n, alone=True):
                    at = (layer * QUARTERS + q) * BODIES * BATCHES + n
                    if alone:
                        held(ga_used, i * BATCHES + (at + AHEAD - 1))
                        for j in range(BATCH):
                            last = nc.scalar.activation(hits[n % 2][:, j * P:(j + 1) * P], keyno, ACT.Abs,
                                                        bias=picks[:, 0, n * BATCH + j:n * BATCH + j + 1])
                        steps(last)
                        nc.scalar.activation(hits[n % 2], hits[n % 2], ACT.Relu, scale=-1.0, bias=1.0).then_inc(hit_ready, 1)
                    if n % 4 == 3:
                        held(ga_used, i * BATCHES + (at + AHEAD + 1))
                        g3 = gates[q % 2].rearrange("p (a t) -> p a t", t=ND)
                        nc.scalar.activation(g3[:, :, bass.ds(i * (BATCH * BATCHES) + n // 4 * 16, 16)],
                                             ps[6 + n // 4].rearrange("p (t a) -> p a t", a=QA), ACT.Copy).then_inc(ga_copied, 1)

                def block_gelu(e, i):
                    at = layer * NKEY + e
                    held(blk_summed, i * BLOCKS + (at + 1))
                    held(blk_done, i * BLOCKS + (at + AHEAD + 1))
                    nc.scalar.activation(zg[e % 4], ps[4 + e % 2][:, 0:ND], ACT.Gelu).then_inc(blk_gelu, 1)

                def group_gelu(g, i):
                    act.wait_ge(act_in, i * STEP_GROUPS + (g + 1))
                    nc.scalar.activation(g8, a8, ACT.Gelu).then_inc(act_out, 1)

                for half in range(2):
                    with act.Fori(0, BODIES // 2) as i:
                        step_picks(i + half * (BODIES // 2))
                        for n in range(BATCHES):
                            spread_batch(0, i + half * (BODIES // 2), n, alone=by_scalar(n))
                    gate_exp(GATHERED[half])
                block_gelu(0, 0)
                block_gelu(1, 0)

                def step_(q, i, last_step=False):
                    if q + 1 < QUARTERS:
                        step_picks(i)
                    for j in range(BLOCKS):
                        e = q * QA + j
                        if not (last_step and j >= BLOCKS - 2):
                            block_gelu(e + 2, i)
                        if q + 1 < QUARTERS:
                            spread_batch(q + 1, i, 2 * j)
                            spread_batch(q + 1, i, 2 * j + 1)
                        if j % 2 == 0:
                            group_gelu((layer * QUARTERS + q) * BODIES * STEP_GROUPS + j // 2, i)

                for q in range(QUARTERS):
                    last = q == QUARTERS - 1
                    with act.Fori(0, BODIES - last) as i:
                        step_(q, i)
                    if last:
                        step_(q, BODIES - 1, True)
                    if layer == 0 and q % 2:
                        seen.next(x_ready)
                        squares(q // 2)
                        root(1)
                if layer == 0:
                    for t in DENSE:
                        seen.next(x_ready)
                        squares(t)
                        root(1)

            act.sem_inc(blk_gelu, AHEAD)
            act.sem_inc(ga_copied, AHEAD)
            queries(0)
            for n in range(NH, 12):
                modulation(n)
            peer_acts(0)

            seen.next(dve_to_act)
            for t in range(NT):
                squares(t)
            root(NT)
            turn_tokens()
            seen.next(dve_to_act)
            nc.scalar.activation(sin, ang, ACT.Sin).then_inc(act_to_dve, 1)
            nc.scalar.activation(cos, ang, ACT.Sin, scale=0.5).then_inc(act_to_dve, 1)
            for dst in (rqT, rkT):
                skip(NT)
                for t in range(NT):
                    turned(dst[:, :, t * P:(t + 1) * P])
            for t in range(NT):
                bank, free = projected()
                nc.scalar.activation(rv[:, t, :], bank, ACT.Copy).then_inc(free, 1)
            for t in range(NT):
                bank, free = projected()
                nc.scalar.activation(rg[:, t, :], bank, ACT.Silu).then_inc(free, 1)
            for dst in (sqT, skT):
                for t in range(NT):
                    bank, free = projected()
                    nc.scalar.activation(sq, bank, ACT.Square).then_inc(ss_done, 1)
                    root(8)
                    if t:
                        turned(dst[:, :, (t - 1) * P:t * P])
                turned(dst[:, :, 3 * P:4 * P])
            for t in range(NT):
                bank, free = projected()
                nc.scalar.activation(sv[:, t, :], bank, ACT.Copy).then_inc(free, 1)
            for h in range(8):
                head_out(h, 64, 0, 8 + h + 1)
            nc.scalar.preload_act_table_set("natural_log_exp_and_others")
            for n in range(8 * NT + 1):
                h, j = n // NT, NT - 1 - n % NT
                if n < 8 * NT:
                    wd = SEQ - j * P
                    z, l = ps[4 + n % 2][:, 0:wd], ab[n % 2][:, 0:wd]
                    act.wait_ge(z_done, 8 * NT + n + 1)
                    if n >= 2:
                        act.wait_ge(z_used, n - 1)
                    step(nc.scalar.activation(l, z, ACT.Abs))
                    step(nc.scalar.activation(l, l, ACT.Exp, scale=-1.0))
                    nc.scalar.activation(l, l, ACT.Ln, bias=1.0).then_inc(ln_ready, 1)
                if n >= 1:
                    m = n - 1
                    h, j = m // NT, NT - 1 - m % NT
                    act.wait_ge(ar_done, m + 1)
                    if j == NT - 1:
                        act.wait_ge(pv_done, 8 + 8 + h - 1)
                    nc.scalar.activation(st1[h % 2][:, j, j * P:SEQ], ps[6 + m % 2][:, 0:SEQ - j * P], ACT.Exp).then_inc(w_exp, 1)
                    if j == 0 and h >= 1:
                        head_out(h - 1, 64, 512, 8 + 8 + h)
            head_out(7, 64, 512, 8 + 8 + 8)
            act.wait_ge(pv_used, 8 + 16)
            squares_of_heads(16)
            mixed_to_queries(1)
            queries(1)
            peer_acts(1)

        @block.vector
        def _(dve):
            seen, step, chosen, spreads = Seen(dve), Chain(dve, c_dve), Chain(dve, c_top), Chain(dve, c_picks)
            n_out = [0]
            tt, ts, stt = nc.vector.tensor_tensor, nc.vector.tensor_scalar, nc.vector.scalar_tensor_tensor

            def spread(v, shape):
                while len(v.shape) < len(shape):
                    v = v.unsqueeze(len(v.shape))
                return v.to_broadcast(shape)

            def projected():
                n = n_out[0]
                n_out[0] += 1
                dve.wait_ge(pj_done, n + 1)
                return ps[n % 2], pj_free[n % 2], n // 2 + 1

            def skip(k):
                n_out[0] += k

            def rstd(n, count):
                ts(var[:, 0:n], ss[:, 0:n], 1.0 / count, EPS, ALU.mult, ALU.add).then_inc(var_ready, 1)
                seen.next(var_ready)
                seen.next(std_ready)
                step(nc.vector.reciprocal(rs[:, 0:n], std[:, 0:n]))
                step(tt(nt_[:, 0:n], rs[:, 0:n], rs[:, 0:n], ALU.mult))
                step(tt(nt_[:, 0:n], nt_[:, 0:n], var[:, 0:n], ALU.mult))
                step(ts(nt_[:, 0:n], nt_[:, 0:n], -0.5, 1.5, ALU.mult, ALU.add))
                step(tt(rs[:, 0:n], rs[:, 0:n], nt_[:, 0:n], ALU.mult))

            def normed(gain, shift=None):
                seen.next(ss_done, NT)
                rstd(NT, D)
                for t in range(NT):
                    last = stt(hn[:, t, :], x[:, t, :], rs[:, t:t + 1], gain, ALU.mult, ALU.mult)
                    if shift is not None:
                        step(last)
                        last = tt(hn[:, t, :], hn[:, t, :], shift, ALU.add)
                    last.then_inc(src_ready, 1)

            step(nc.vector.memset(ones, 1.0))
            dve.wait_ge(row_in, 32)
            normed(rows[:, 0, :])
            seen.next(act_to_dve)
            dve.wait_ge(cst_in, 16 * 14)
            step(tt(lb3[:, 2, :], lb3[:, 0, :], lb3[:, 1, :], ALU.max))
            step(tt(lb3[:, 0, :], lb3[:, 0, :], lb3[:, 2, :], ALU.subtract))
            tt(lb3[:, 1, :], lb3[:, 1, :], lb3[:, 2, :], ALU.subtract).then_inc(dve_to_act, 1)
            seen.next(act_to_dve)
            step(tt(lb3[:, 4, :], lb3[:, 4, :], lb3[:, 3, :], ALU.add))
            step(nc.vector.reciprocal(lb3[:, 4, :], lb3[:, 4, :]))
            step(tt(lb3[:, 4, :], lb3[:, 3, :], lb3[:, 4, :], ALU.mult))
            step(ts(lb3[:, 5, :], lb3[:, 4, :], -1.0, 1.0, ALU.mult, ALU.add))

            skip(4)
            for c in range(4):
                n = 4 + c
                dve.wait_ge(pj_free[n % 2], n // 2 + 1)
                step(ts(cum[:, c, :], kT[:, c, :], lb3[:, 5, c:c + 1], lb3[:, 4, c:c + 1], ALU.mult, ALU.add))
                ts(kT[:, c, :], cum[:, c, :], -1.0, 1.0, ALU.mult, ALU.add).then_inc(dve_to_act, 1)
            for c in range(4):
                seen.next(act_to_dve)
                step(nc.vector.tensor_tensor_scan(cum[:, c, :], reset, qk[c], 0.0, ALU.mult, ALU.add))
            for c in range(2):
                dve.wait_ge(low_done, 2)
                ts(cum[:, 4 + c, :], ps[5 + c], bg[:, c:c + 1], None, ALU.add).then_inc(dve_to_act, 1)
            for c in range(2):
                seen.next(act_to_dve)
                step(stt(qk[4 + c], cum[:, 4 + c, :], 0.0, qk[4 + c], ALU.min, ALU.subtract))
                step(nc.vector.tensor_tensor_scan(cum[:, 4 + c, :], reset, qk[4 + c], 0.0, ALU.mult, ALU.add))
            step(nc.vector.tensor_copy(tot.rearrange("p (g c) -> p g c", g=6),
                                       cum.rearrange("p g (c s) -> p g c s", s=CHUNK)[:, :, :, CHUNK - 1]))
            step(nc.vector.memset(rows[:, 2, 512:512 + 144], 0.0))
            T = tot.rearrange("p (g m c) -> p (g m) c", g=6, c=4)
            T8 = tot.rearrange("p (g c) -> p g c", g=6)
            o0 = offs[:, 0].rearrange("p g (m c) -> p (g m) c", c=4)
            o1 = offs[:, 1].rearrange("p g (m c) -> p (g m) c", c=4)
            o2 = offs[:, 2]
            cp = nc.vector.tensor_copy
            step(cp(o0[:, :, 0], T[:, :, 0]))
            step(cp(o0[:, :, 2], T[:, :, 2]))
            step(cp(o1[:, :, 1], T[:, :, 1]))
            step(tt(o1[:, :, 0], T[:, :, 0], T[:, :, 1], ALU.add))
            step(ts(o1[:, :, 3], T[:, :, 2], -1.0, None, ALU.mult))
            step(cp(o2[:, :, 3], T8[:, :, 3]))
            for c in (2, 1, 0):
                step(tt(o2[:, :, c], o2[:, :, c + 1], T8[:, :, c], ALU.add))
            for c in (5, 6, 7):
                step(tt(o2[:, :, c], o2[:, :, c - 1], T8[:, :, c - 1], ALU.subtract))

            FAR = (64, 128, 256)
            spans = (256, 128) + IN_TILE
            assert len(spans) == NQK and spans[2] == 64

            def halves(v, s):
                w = v.rearrange("p (m r s) -> p m r s", r=2, s=s)
                return w[:, :, 0, :], w[:, :, 1, :]

            def exponents(g, l, e):
                s = spans[l]
                if s >= CHUNK:
                    k = s // CHUNK
                    cv = cum[:, g, :].rearrange("p (m r k s) -> p m r k s", r=2, k=k, s=CHUNK)
                    ev = e.rearrange("p (m r k s) -> p m r k s", r=2, k=k, s=CHUNK)
                    ov = offs[:, FAR.index(s), g, :].rearrange("p (m r k) -> p m r k", r=2, k=k)
                    m = SEQ // (2 * s)
                    for r in range(2):
                        o = spread(ov[:, :, r, :], [P, m, k, CHUNK])
                        c = cv[:, :, r, :, :]
                        last = tt(ev[:, :, r, :, :], *((c, o) if r else (o, c)), ALU.subtract)
                    return last
                (ce, co), (ee, eo) = halves(cum[:, g, :], s), halves(e, s)
                edge = spread(ce[:, :, s - 1], [P, SEQ // (2 * s), s])
                tt(ee, edge, ce, ALU.subtract)
                return tt(eo, co, edge, ALU.subtract)

            n_ex = 0

            def decayed(g, l, e):
                seen.next(ex_done)
                (ee, eo), (qe, qo) = halves(e, spans[l]), halves(qk[l], spans[l])
                tt(qe, ee, halves(kT[:, g, :], spans[l])[0], ALU.mult)
                tt(qo, eo, halves(qT[:, g, :], spans[l])[1], ALU.mult).then_inc(qk_ready, 1)

            h = 0
            for g in range(6):
                for l in range(NQK + 1):
                    if l < NQK:
                        if n_ex + l >= 3:
                            dve.wait_ge(qk_ready, n_ex + l - 2)
                        exponents(g, l, ex[(n_ex + l) % 3]).then_inc(ex_sub, 1)
                    if l >= 1:
                        decayed(g, l - 1, ex[(n_ex + l - 1) % 3])
                n_ex += NQK
                for _ in range(1 if g < 4 else 2):
                    for t in range(NT):
                        n = h * NT + t
                        dve.wait_ge(lev_done, n + 1)
                        if t == 0 and h >= 2:
                            dve.wait_ge(pv_done, h - 1)
                        b = 4 + 2 * (n % 2)
                        if n >= 1:
                            dve.wait_ge(st_ready, n)
                        tt(mk, psum[:, b * 512:(b + 2) * 512], levels, ALU.mult).then_inc(lev_used, 1)
                        dve.wait_ge(lev_used, n + 1)
                        nc.vector.tensor_reduce(st1[h % 2][:, t, t * P:(t + 1) * P], mk.rearrange("p (l i) -> p i l", l=NLEV),
                                                AX_X, ALU.add).then_inc(st_ready, 1)
                    h += 1

            def by_head(v, n, width):
                return v.rearrange("p (h n) -> p h n", n=width), [P, n, width]

            dve.wait_ge(pv_used, 8)
            for t in range(NT):
                hv, shape = by_head(hn[:, t, :], 8, P)
                seen.next(ss_done)
                step(nc.vector.tensor_reduce(ss[:, 0:8], by_head(scr[t % 2], 8, P)[0], AX_X, ALU.add))
                rstd(8, P)
                step(tt(hv, hv, spread(rs[:, 0:8], shape), ALU.mult))
                for m in range(2):
                    half = hn[:, t, m * 512:(m + 1) * 512]
                    g = srow[:, m * P:(m + 1) * P].unsqueeze(1).to_broadcast([P, 4, P])
                    step(tt(by_head(half, 4, P)[0], by_head(half, 4, P)[0], g, ALU.mult))
                    last = tt(half, half, sg1[:, m, t, :], ALU.mult)
                last.then_inc(src_ready, 1)
            skip(24)
            assert n_out[0] == before[7], (n_out, before[7])
            for s in range(2):
                for t in range(NT):
                    bank, free, _ = projected()
                    xs = x[:, t, s * SEC:(s + 1) * SEC]
                    tt(xs, xs, bank, ALU.add).then_inc(free, 1)
            normed(rows[:, 1, :])

            def peer(layer):
                skip(16)
                by_tile = s_all.rearrange("p (t m n) -> p t m n", t=NT, m=2 * NH)
                with dve.Fori(0, NH // 2) as h:
                    chosen.restart()
                    for m in range(4):
                        dve.wait_ge(sc_done, h * 4 + (2 * NH * layer + m + 1))
                        nc.vector.tensor_copy(by_tile[:, :, bass.ds(h * 4 + m, 1), :],
                                              ps[4 + m].rearrange("p (t m n) -> p t m n", t=NT, m=1)).then_inc(sc_used, 1)
                    dve.wait_ge(sc_used, h * 4 + (2 * NH * layer + 4))
                    for t in DENSE:
                        head_experts(t, h, chosen)
                for n, t in enumerate(DENSE):
                    if n:
                        dve.wait_ge(picks_turned, len(DENSE) * layer + n)
                    numbers_and_gates(t)
                dve.wait_ge(picks_turned, len(DENSE) * (layer + 1))
                dve.wait_ge(picks_copied, layer + 1)

                def step_tokens(i, n=0):
                    return bass.ds(i * (2 * HALF) + n * BATCH, HALF)

                def spread_half(q, i, n):
                    at = (layer * QUARTERS + q) * BODIES * BATCHES + n
                    dve.wait_ge(ga_used, i * BATCHES + (at + AHEAD - 4))
                    g, shape = ga[n // 4], [P, HALF, QA]
                    keys = keyno[:, q * QA:(q + 1) * QA].unsqueeze(1).to_broadcast(shape)
                    spreads(tt(g, keys, spread(iaT[:, step_tokens(i, n)], shape), ALU.is_equal))
                    tt(g, g, spread(gT[:, step_tokens(i, n)], shape), ALU.mult).then_inc(ga_ready, 1)

                def one_hot_keys(i, n):
                    at = layer * QUARTERS * BODIES * BATCHES + n
                    dve.wait_ge(ga_used, i * BATCHES + (at + AHEAD - 1))
                    for j in range(BATCH):
                        last = ts(hits[n % 2][:, j * P:(j + 1) * P], keyno, picks[:, 1, n * BATCH + j:n * BATCH + j + 1], 0.0,
                                  ALU.add, ALU.is_equal)
                    last.then_inc(hit_by_vector, 1)

                for n, t in enumerate(GATHERED):
                    with dve.Fori(0, BODIES // 2) as h:
                        chosen.restart()
                        spreads.restart()
                        now = h + n * (BODIES // 2)
                        spreads(nc.vector.tensor_copy(picks[:, 1, :], nibT[:, bass.ds(now * (BATCH * BATCHES), BATCH * BATCHES)]))
                        batches = iter(range(BATCHES))

                        def between():
                            b = next(batches, None)
                            if b is None:
                                return
                            if b % 4 == 0:
                                spread_half(0, now, b)
                            if not by_scalar(b):
                                one_hot_keys(now, b)
                        head_experts(t, h, chosen, between)
                        assert next(batches, None) is None
                    numbers_and_gates(t)
                step(nc.vector.memset(zero_row, 0.0))
                dve.sem_inc(all_chosen, 1)

                def weigh_block(q, j, i):
                    at = layer * NKEY + q * QA + j
                    dve.wait_ge(blk_gelu, i * BLOCKS + (at + AHEAD + 1))
                    z = zg[j % 4]
                    tt(z, z, gates[q % 2][:, bass.ds(i * (BLOCKS * ND) + j * ND, ND)], ALU.mult).then_inc(blk_ready, 1)

                for q in range(QUARTERS):
                    t = q // 2
                    if q % 2 == 0:
                        dve.wait_ge(ada_stored, 16 * 12)
                        step(nc.vector.memset(y, 0.0))
                    dve.wait_ge(ga_copied, AHEAD + (layer * QUARTERS + q + 1) * BODIES * 2)
                    with dve.Fori(0, BODIES) as i:
                        if q + 1 < QUARTERS:
                            spreads.restart()
                        for g in range(STEP_GROUPS):
                            at = (q % 2) * BODIES * STEP_GROUPS + g

                            def meanwhile(j):
                                weigh_block(q, j, i)
                                if q + 1 < QUARTERS and j % 2 == 0:
                                    spread_half(q + 1, i, 2 * j)
                            group(layer, t, at, i, lambda: meanwhile(2 * g))
                            meanwhile(2 * g + 1)
                    if q % 2:
                        finish_tile(layer, t, y)
                dve.wait_ge(dense_done, layer + 1)
                for n, t in enumerate(DENSE):
                    finish_tile(layer, t, y_dense[n])

            def top16(step, rows_, between):
                v, lag = nc.vector, len(rows_) - 1
                for src, values, places in rows_:
                    step(v.max(values[:, 0:8], src), lag)
                between()
                for src, values, places in rows_:
                    step(v.max_index(places[:, 0:8], values[:, 0:8], src), lag)
                for src, values, places in rows_:
                    step(v.match_replace(src, values[:, 0:8], src, NEG), lag)
                between()
                for src, values, places in rows_:
                    step(v.max(values[:, 8:16], src), lag)
                for src, values, places in rows_:
                    step(v.max_index(places[:, 8:16], values[:, 8:16], src), lag)
                between()

            def head_experts(t, h, step, between=lambda: None):
                step(nc.vector.tensor_copy(stage.rearrange("p s n -> p (s n)"), s_all[:, bass.ds(h * 512 + t * 2048, 512)]))
                between()
                top16(step, [(stage[:, m, :], tv[:, m, :], ti[:, m * TOPK:(m + 1) * TOPK]) for m in range(4)], between)
                for n in range(2):
                    if n == 0:
                        all_done(step)
                    step(tt(cand[:, n, :].rearrange("p (a b) -> p a b", a=TOPK), spread(tv[:, 2 * n, :], [P, TOPK, TOPK]),
                            tv[:, 2 * n + 1, :].unsqueeze(1).to_broadcast([P, TOPK, TOPK]), ALU.add), 1)
                between()
                top16(step, [(cand[:, n, :], hb[:, n * TOPK:(n + 1) * TOPK], hp[:, n * TOPK:(n + 1) * TOPK]) for n in range(2)],
                      between)
                all_done(step)
                hb3, out3 = [v.rearrange("p (h k) -> p h k", h=2) for v in (hb, bv[t][:, bass.ds(h * (2 * TOPK), 2 * TOPK)])]
                step(nc.vector.tensor_copy(tif[t][:, bass.ds(h * (4 * TOPK), 4 * TOPK)], ti), 2)
                step(nc.vector.tensor_copy(bp[t][:, bass.ds(h * (2 * TOPK), 2 * TOPK)], hp), 2)
                step(tt(out3, hb3, hb3[:, :, 0:1].to_broadcast([P, 2, TOPK]), ALU.subtract))

            def all_done(step):
                step.eng.wait_ge(step.sem, step.n)

            def numbers_and_gates(t):
                oh3 = onehot.rearrange("p (s k) -> p s k", k=TOPK)
                oh4 = onehot.rearrange("p (h s k) -> p h s k", h=NH, k=TOPK)
                ti4 = tif[t].rearrange("p (h s k) -> p h s k", h=NH, s=2)
                it = iota.unsqueeze(1).to_broadcast([P, SLOTS, TOPK])
                gt = gate[:, t * SLOTS:(t + 1) * SLOTS]
                gt3 = gt.rearrange("p (h k) -> p h k", k=TOPK)
                nc.vector.tensor_copy(gt, bv[t]).then_inc(dve_to_act, 1)
                for m, dst in ((0, ia), (1, ib)):
                    if m == 0:
                        step(ts(pai, bp[t], 4, None, ALU.logical_shift_right))
                    else:
                        step(ts(pai, bp[t], 15, None, ALU.bitwise_and))
                    step(nc.vector.tensor_copy(paf, pai))
                    step(tt(oh3, spread(paf, [P, SLOTS, TOPK]), it, ALU.is_equal))
                    step(tt(oh4, oh4, ti4[:, :, m, :].unsqueeze(2).to_broadcast([P, NH, TOPK, TOPK]), ALU.mult))
                    step(nc.vector.tensor_reduce(dst, oh3, AX_X, ALU.add))
                if t in GATHERED:
                    step(stt(idf, ia, float(NKEY), ib, ALU.mult, ALU.add))
                    step(nc.vector.tensor_copy(idx[:, t * SLOTS:(t + 1) * SLOTS], idf))
                seen.next(act_to_dve)
                step(nc.vector.tensor_reduce(ss[:, 0:NH], gt3, AX_X, ALU.add))
                step(nc.vector.reciprocal(rs[:, 0:NH], ss[:, 0:NH]))
                step(tt(gt3, gt3, spread(rs[:, 0:NH], [P, NH, TOPK]), ALU.mult))
                dve.sem_inc(picks_ready if t in DENSE else top_ready, 1)

            def group(layer, t, at, i, meanwhile):
                base = (layer * len(GATHERED) + t) * GROUPS + at
                for b in range(RING):
                    dve.wait_ge(u_in[b], i * (16 * STEP_GROUPS) + 16 * (base + 1))
                    nc.vector.tensor_tensor_reduce(out=ur[b], in0=ur[b], in1=hn[:, t, :], scale=1.0, scalar=0.0,
                                                   op0=ALU.mult, op1=ALU.add, accum_out=a8[:, b:b + 1])\
                        .then_inc(u_free, 1)
                dve.wait_ge(u_free, i * (RING * STEP_GROUPS) + (RING * (base + 2)))
                dve.sem_inc(act_in, 1)
                meanwhile()
                dve.wait_ge(act_out, i * STEP_GROUPS + (base + 1))
                nc.vector.tensor_tensor(c8, g8, gate[:, bass.ds(i * (RING * STEP_GROUPS) + (t * SLOTS + at * RING), RING)], ALU.mult)\
                    .then_inc(c8_ready, 1)
                dve.wait_ge(c8_ready, i * STEP_GROUPS + (base + 1))
                for b in range(RING):
                    dve.wait_ge(v_in[b], i * (16 * STEP_GROUPS) + 16 * (base + 1))
                    stt(y, vr[b], c8[:, b:b + 1], y, ALU.mult, ALU.add).then_inc(v_free, 1)
                    dve.wait_ge(v_free, i * (RING * STEP_GROUPS) + (RING * (base + 1) + b + 1))

            def finish_tile(layer, t, y):
                if layer == 0:
                    tt(x[:, t, :], x[:, t, :], y, ALU.add).then_inc(x_ready, 1)
                    dve.wait_ge(x_ready, t + 1)
                    seen.next(ss_done)
                    if t:
                        step(nc.vector.tensor_copy(ss[:, 0:1], ss[:, t:t + 1]))
                    rstd(1, D)
                    step(stt(x[:, t, :], x[:, t, :], rs[:, 0:1], rows[:, 2, :], ALU.mult, ALU.mult))
                else:
                    step(tt(ysum, y, mod[:, 5, :], ALU.mult))
                    tt(x[:, t, :], x[:, t, :], ysum, ALU.add).then_inc(out_ready, 1)
                    dve.wait_ge(out_ready, t + 1)

            dve.sem_inc(u_free, RING)
            dve.sem_inc(v_free, RING)
            peer(0)
            dve.sem_inc(dve_to_act, 1)

            dve.wait_ge(first_in, 32)
            step(stt(rows[:, 0, :], mod[:, 1, :], 1.0, rows[:, 0, :], ALU.add, ALU.mult))
            normed(rows[:, 0, :], mod[:, 0, :])
            step(nc.vector.tensor_copy(posf, pos))
            for t in range(NT):
                step(ts(ang[:, t, :], freq, posf[:, t:t + 1], None, ALU.mult))
            step(ts(turn, ang, 1.0 / TWO_PI, ROUND, ALU.mult, ALU.add))
            step(ts(turn, turn, -ROUND, None, ALU.add))
            for c in two_pi:
                step(stt(ang, turn, -c, ang, ALU.mult, ALU.add))
            ts(ang, ang, 3.1415925, -3.1415925, ALU.min, ALU.max).then_inc(dve_to_act, 1)
            seen.next(act_to_dve)
            step(ts(nsin, sin, -1.0, None, ALU.mult))
            seen.next(act_to_dve)
            step(tt(cos, cos, cos, ALU.mult))
            dve.wait_ge(row_in, 16 * 8)
            dve.wait_ge(mod_in, 16)
            step(stt(rows[:, 1, :], mod[:, 4, :], 1.0, rows[:, 1, :], ALU.add, ALU.mult))
            step(ts(srow[:, 512:576], srow[:, 512:576], 64 ** -0.5, None, ALU.mult))
            step(ts(cos, cos, -2.0, 1.0, ALU.mult, ALU.add))
            n_rt = 0
            for m in range(2):
                for t in range(NT):
                    bank, free, count = projected()
                    if n_rt >= 2:
                        dve.wait_ge(tr_done, 32 + n_rt - 1)
                    dve.wait_ge(src_ready, 4 * NT + n_rt)
                    r = rt[n_rt % 2]
                    n_rt += 1
                    r4, b4, t4 = [v.rearrange("p (h r n) -> p h r n", h=8, r=2) for v in (r, bank, t3)]
                    tt(r4, b4, cos[:, t, :].unsqueeze(1).unsqueeze(1).to_broadcast([P, 8, 2, 32]), ALU.mult)
                    tt(t4[:, :, 0, :], b4[:, :, 1, :], nsin[:, t, :].unsqueeze(1).to_broadcast([P, 8, 32]), ALU.mult)
                    tt(t4[:, :, 1, :], b4[:, :, 0, :], sin[:, t, :].unsqueeze(1).to_broadcast([P, 8, 32]), ALU.mult)\
                        .then_inc(free, 1)
                    dve.wait_ge(free, count)
                    tt(r, r, t3, ALU.add).then_inc(src_ready, 1)
            skip(2 * NT)
            for m in range(2):
                for t in range(NT):
                    bank, free, count = projected()
                    seen.next(ss_done)
                    step(nc.vector.tensor_reduce(ss[:, 0:8], by_head(sq, 8, 64)[0], AX_X, ALU.add))
                    rstd(8, 64)
                    dve.wait_ge(tr_done, 32 + n_rt - 1)
                    dve.wait_ge(src_ready, 4 * NT + n_rt)
                    r = rt[n_rt % 2]
                    n_rt += 1
                    r3, shape = by_head(r, 8, 64)
                    tt(r3, by_head(bank, 8, 64)[0], spread(rs[:, 0:8], shape), ALU.mult).then_inc(free, 1)
                    dve.wait_ge(free, count)
                    g = srow[:, 512 + 64 * m:576 + 64 * m].unsqueeze(1).to_broadcast(shape)
                    tt(r3, r3, g, ALU.mult).then_inc(src_ready, 1)
            skip(NT)
            for h in range(8):
                dve.wait_ge(dec_in[h % 2], 16 * (h // 2 + 1))
                if h >= 2:
                    dve.wait_ge(pv_done, 8 + h - 1)
                for j in range(NT):
                    n = h * NT + j
                    dve.wait_ge(z_done, n + 1)
                    wd = SEQ - j * P
                    tt(st1[h % 2][:, j, j * P:SEQ], ps[4 + n % 4][:, 0:wd], dec[h % 2][:, 0:wd], ALU.mult).then_inc(wt_ready, 1)
            def centred(t):
                rv_, rshape = by_head(hn[:, t, 0:512], 8, 64)
                step(nc.vector.tensor_reduce(ss[:, 16:24], rv_, AX_X, ALU.add))
                step(ts(ss[:, 16:24], ss[:, 16:24], 1.0 / 64, None, ALU.mult))
                tt(rv_, rv_, spread(ss[:, 16:24], rshape), ALU.subtract).then_inc(dve_to_act, 1)
                step(tt(rg[:, t, :], rg[:, t, :], srow[:, 0:512], ALU.mult))

            for n in range(8 * NT + 1):
                if n % 8 == 5:
                    dve.wait_ge(pv_used, 8 + 8)
                    centred(n // 8)
                if n < 8 * NT:
                    h, j = n // NT, NT - 1 - n % NT
                    wd = SEQ - j * P
                    dve.wait_ge(ln_ready, n + 1)
                    if j == NT - 1:
                        if h >= 2:
                            dve.wait_ge(ar_done, NT * (h - 1))
                        else:
                            dve.wait_ge(z_done, 8 * NT + 1)
                    sv_ = stay[h % 2][:, j, j * P:SEQ]
                    stt(sv_, ps[4 + n % 2][:, 0:wd], 0.0, ab[n % 2][:, 0:wd], ALU.max, ALU.add).then_inc(z_used, 1)
                    dve.wait_ge(z_used, n + 1)
                    sv_ = stay[h % 2][:, j, j * P:(j + 1) * P]
                    tt(sv_, sv_, sticks[:, 2, :], ALU.mult).then_inc(sp_ready, 1)
                if n >= 1:
                    h, j = (n - 1) // NT, NT - 1 - (n - 1) % NT
                    dve.wait_ge(w_exp, n)
                    wv = st1[h % 2][:, j, j * P:(j + 1) * P]
                    tt(wv, wv, sticks[:, 2, :], ALU.mult).then_inc(wt_ready, 1)
            dve.wait_ge(pv_used, 8 + 16)
            for t in range(NT):
                hv, shape = by_head(hn[:, t, :], 16, 64)
                seen.next(ss_done)
                step(nc.vector.tensor_reduce(ss[:, 0:16], by_head(scr[t % 2], 16, 64)[0], AX_X, ALU.add))
                rstd(16, 64)
                step(tt(hv, hv, spread(rs[:, 0:16], shape), ALU.mult))
                tt(hn[:, t, 0:512], hn[:, t, 0:512], rg[:, t, :], ALU.mult)
                sh, sshape = by_head(hn[:, t, 512:1024], 8, 64)
                tt(sh, sh, srow[:, 640:704].unsqueeze(1).to_broadcast(sshape), ALU.mult).then_inc(src_ready, 1)
            for s in range(2):
                for t in range(NT):
                    bank, free, count = projected()
                    cs = slice(s * SEC, (s + 1) * SEC)
                    step(tt(t3, bank, mod[:, 2, cs], ALU.mult))
                    tt(x[:, t, cs], x[:, t, cs], t3, ALU.add).then_inc(free, 1)
                    dve.wait_ge(free, count)
            normed(rows[:, 1, :], mod[:, 3, :])
            peer(1)

        @block.gpsimd
        def _(pool):
            pool.wait_ge(ada_done, 12)
            for layer in range(2):
                for t in GATHERED:
                    base = (layer * len(GATHERED) + t) * GROUPS
                    chosen = layer * len(GATHERED) + t + 1
                    pool.wait_ge(top_ready, chosen)
                    with pool.Fori(0, GROUPS // 2) as i:
                        for j in range(2):
                            slot_free = [pool.to_reg(i * (2 * RING) + ((base + j) * RING + b + 1)) for b in range(RING)]
                            nc.gpsimd.tensor_copy(i8[j], idx[:, bass.ds(i * (2 * RING) + (t * SLOTS + j * RING), RING)])\
                                .then_inc(c_pool, 1)
                            copied = pool.to_reg(i * 2 + (base + j + 1))
                            pool.wait_ge(top_ready, chosen)
                            pool.wait_ge(c_pool, copied)
                            for table, ring, free, landed in ((layer_u, ur, u_free, u_in), (layer_v, vr, v_free, v_in)):
                                for b in range(RING):
                                    pool.wait_ge(top_ready, chosen)
                                    pool.wait_ge(free, slot_free[b])
                                    nc.gpsimd.indirect_dma_start(ring[b], None, table[layer],
                                                                 bass.IndirectOffsetOnAxis(i8[j][:, b:b + 1], 0))\
                                        .then_inc(landed[b], 16)


_INPUTS = ["x", "norm1_g", "w_in", "hg_lower_logits", "hg_norm_g", "gla_w_gate_up", "gla_b_gate", "gla_norm_g", "w_out",
           "norm2_g", "peer_w_q", "peer_u", "peer_v", "norm_f_g", "c_2", "positions_2", "ada_w_2", "ada_b_2",
           "norm1_gain_2", "norm2_gain_2", "w_in_2", "ret_norm_gain_2", "sb_q_gain_2", "sb_k_gain_2", "sb_out_gain_2",
           "w_out_2", "peer_w_query_2", "peer_down_2", "peer_up_2"]


def kernel(**inputs):
    import concourse.bacc as bacc
    from concourse.bass_utils import run_bass_kernel_spmd

    consts, two_pi = constants()
    data = {}
    for name in _INPUTS:
        v = np.ascontiguousarray(inputs[name])
        if name != "norm_f_g" and name != "hg_lower_logits" and v.shape[0] == 1:
            v = v[0]
        data[name] = v
    for name, key in (("peer_sub_keys", "keysT"), ("peer_sub_keys_2", "keysT_2")):
        data[key] = np.ascontiguousarray(np.asarray(inputs[name])[0].transpose(3, 0, 1, 2).reshape(P, 16 * NKEY))
    for name, key in (("peer_u", "uT"), ("peer_down_2", "uT_2")):
        data[key] = np.ascontiguousarray(data[name].reshape(NKEY, NKEY, KC, P).transpose(3, 0, 2, 1).reshape(P, NKEY * D))
    data.update(consts)
    nc = bacc.Bacc("TRN2", target_bir_lowering=False, num_devices=1)
    aps = {k: nc.dram_tensor(f"in_{k}", v.shape, mybir.dt.from_np(v.dtype), kind="ExternalInput").ap() for k, v in data.items()}
    out = nc.dram_tensor("out_y", (SEQ, D), F32, kind="ExternalOutput").ap()
    mod_dram = nc.dram_tensor("modulation", (1, 6 * D), F32, kind="Internal").ap()
    build(nc, aps, out, mod_dram, two_pi)
    r = run_bass_kernel_spmd(nc, [{f"in_{k}": v for k, v in data.items()}], core_ids=[0])
    return r.results[0]["out_y"].reshape(1, SEQ, D)
```
